# Optimizing a Trainium2 kernel written in Bass

```python
import jax
import jax.numpy as jnp
from jax import lax
import numpy as np

D_MODEL = 1024
BATCH = 1
SEQ = 256
DEPTH = 2

CHUNK = 64
HEAD_DIM = 64
SWA_HEADS = 8
SWA_KV_HEADS = 2
SWA_WINDOW = 128
WINDOW_CHUNKS = SWA_WINDOW // CHUNK
NUM_BUCKETS = 32
MAX_DISTANCE = 128
GLA_HEADS = 4
GLA_DK = 64
GLA_DV = 128
GLA_GATE_RANK = 16
GLA_GATE_TAU = 16.0
CONV_CH = 512
CONV_K = 3
BRANCH_WIDTH = 512
N_BRANCH = 3
MEM_LEN = 256
X_HEADS = 4
X_HEAD_DIM = D_MODEL // X_HEADS
DENSE_FF = 2816
N_EXPERTS = 8
TOP_K = 2
EXPERT_FF = 3584
MOE_BLOCK = 128
N_DENSE = (DEPTH + 1) // 2
N_MOE = DEPTH // 2
LN_EPS = 1e-5
DEEPNORM_ALPHA = (2 * DEPTH) ** 0.25
DEEPNORM_BETA = (8 * DEPTH) ** -0.25

IN_SPLITS = [SWA_HEADS * HEAD_DIM, SWA_KV_HEADS * HEAD_DIM, SWA_KV_HEADS * HEAD_DIM,
             GLA_HEADS * GLA_DK, GLA_HEADS * GLA_DK, GLA_HEADS * GLA_DV, GLA_HEADS * GLA_DV, GLA_GATE_RANK,
             CONV_CH, CONV_CH, CONV_CH,
             N_BRANCH * D_MODEL]
D_IN = sum(IN_SPLITS)
IN_OFFSETS = tuple(sum(IN_SPLITS[:i + 1]) for i in range(len(IN_SPLITS) - 1))

kernel_name = 'hybrid_gated_swa_gla_conv_moe_deepnorm'

def layer_norm(x, g, b):
    xf = x.astype(jnp.float32)
    mu = jnp.mean(xf, -1, keepdims=True)
    var = jnp.mean(jnp.square(xf - mu), -1, keepdims=True)
    return ((xf - mu) * lax.rsqrt(var + LN_EPS) * g + b).astype(x.dtype)

def t5_bucket(rel):
    nb = NUM_BUCKETS // 2
    max_exact = nb // 2
    ret = (rel > 0).astype(np.int32) * nb
    n = np.abs(rel)
    large = max_exact + (np.log(np.maximum(n, 1) / max_exact) / np.log(MAX_DISTANCE / max_exact)
                         * (nb - max_exact)).astype(np.int32)
    large = np.minimum(large, nb - 1)
    return ret + np.where(n < max_exact, n, large)

def rel_position_bias(table):
    i = np.arange(CHUNK)[:, None]
    j = np.arange(WINDOW_CHUNKS * CHUNK)[None, :]
    buckets = t5_bucket(j - (WINDOW_CHUNKS - 1) * CHUNK - i)
    return jnp.transpose(table[jnp.asarray(buckets)], (2, 0, 1)).astype(jnp.float32)

def swa_sink_attention(q, k, v, sink, pos_bias):
    B, S, H, hd = q.shape
    KV = k.shape[2]
    G = H // KV
    nc = S // CHUNK
    W = WINDOW_CHUNKS
    qc = q.reshape(B, nc, CHUNK, KV, G, hd)

    def band(t):
        tc = t.reshape(B, nc, CHUNK, KV, hd)
        tp = jnp.pad(tc, ((0, 0), (W - 1, 0), (0, 0), (0, 0), (0, 0)))
        return jnp.concatenate([tp[:, w:w + nc] for w in range(W)], axis=2)

    kb, vb = band(k), band(v)
    s = jnp.einsum('bcqhgd,bckhd->bchgqk', qc, kb).astype(jnp.float32) * (hd ** -0.5)
    s = s + pos_bias.reshape(KV, G, CHUNK, W * CHUNK)
    key_chunk = jnp.arange(nc)[:, None] - (W - 1) + jnp.arange(W * CHUNK)[None, :] // CHUNK
    valid = key_chunk >= 0
    s = jnp.where(valid[None, :, None, None, None, :], s, -1e30)
    sink_col = jnp.broadcast_to(sink.astype(jnp.float32).reshape(KV, G, 1, 1), s.shape[:-1] + (1,))
    p = jax.nn.softmax(jnp.concatenate([s, sink_col], axis=-1), axis=-1)[..., :-1]
    o = jnp.einsum('bchgqk,bckhd->bcqhgd', p.astype(vb.dtype), vb)
    return o.reshape(B, S, H * hd)

def gla_chunk_state(q, k, v, log_a):
    B, S, H, dk = q.shape
    dv = v.shape[-1]
    nc = S // CHUNK
    qc, kc, ac = [t.reshape(B, nc, CHUNK, H, dk) for t in (q, k, log_a)]
    vc = v.reshape(B, nc, CHUNK, H, dv)
    g = jnp.cumsum(ac, axis=2)
    g_end = g[:, :, -1]
    u = jnp.einsum('bcshk,bcshv->bchkv', kc * jnp.exp(g_end[:, :, None] - g), vc)
    decay = jnp.exp(g_end)

    def step(state, inp):
        d, uc = inp
        state = d[..., None] * state + uc
        return state, state

    _, states = lax.scan(step, jnp.zeros((B, H, dk, dv), jnp.float32),
                         (jnp.moveaxis(decay, 1, 0), jnp.moveaxis(u, 1, 0)))
    states = jnp.moveaxis(states, 0, 1)
    o = jnp.einsum('bcshk,bchkv->bcshv', qc, states)
    return o.reshape(B, S, H, dv)

def causal_depthwise_conv(u, w):
    C = u.shape[-1]
    return lax.conv_general_dilated(u, w[:, None, :].astype(u.dtype), window_strides=(1,),
                                    padding=[(CONV_K - 1, 0)],
                                    dimension_numbers=('NWC', 'WIO', 'NWC'),
                                    feature_group_count=C)

def hybrid_mixer(x, w_in, b_merge, sink, pos_bias, w_alpha2, b_alpha2, gla_gain, conv_w, w_branch, w_out):
    B, S, _ = x.shape
    (aq, ak, av, bq, bk, bv, br, blr, cb, cc, ch, gate) = jnp.split(x @ w_in, IN_OFFSETS, axis=-1)
    y_a = swa_sink_attention(aq.reshape(B, S, SWA_HEADS, HEAD_DIM),
                             ak.reshape(B, S, SWA_KV_HEADS, HEAD_DIM),
                             av.reshape(B, S, SWA_KV_HEADS, HEAD_DIM), sink, pos_bias)
    log_a = jax.nn.log_sigmoid((blr @ w_alpha2 + b_alpha2).astype(jnp.float32)) / GLA_GATE_TAU
    o = gla_chunk_state(bq.astype(jnp.float32).reshape(B, S, GLA_HEADS, GLA_DK) * (GLA_DK ** -0.5),
                        bk.astype(jnp.float32).reshape(B, S, GLA_HEADS, GLA_DK),
                        bv.astype(jnp.float32).reshape(B, S, GLA_HEADS, GLA_DV),
                        log_a.reshape(B, S, GLA_HEADS, GLA_DK))
    o = o * lax.rsqrt(jnp.mean(o * o, -1, keepdims=True) + LN_EPS)
    y_b = jax.nn.silu(br) * (o.reshape(B, S, GLA_HEADS * GLA_DV) * gla_gain).astype(x.dtype)
    y_c = cb * causal_depthwise_conv(cc * ch, conv_w)
    gates = jax.nn.sigmoid(gate.reshape(B, S, N_BRANCH, D_MODEL) + b_merge)
    merged = gates[:, :, 0] * (y_a @ w_branch[0])
    merged = merged + gates[:, :, 1] * (y_b @ w_branch[1])
    merged = merged + gates[:, :, 2] * (y_c @ w_branch[2])
    return merged @ w_out

def cross_attention(x, mem, w_q, w_kv, w_o):
    B, S, _ = x.shape
    M = mem.shape[1]
    q = (x @ w_q).reshape(B, S, X_HEADS, X_HEAD_DIM)
    k, v = jnp.split((mem @ w_kv).reshape(B, M, 2, X_HEADS, X_HEAD_DIM), 2, axis=2)
    k, v = k[:, :, 0], v[:, :, 0]
    s = jnp.einsum('bshd,bmhd->bhsm', q, k).astype(jnp.float32) * (X_HEAD_DIM ** -0.5)
    p = jax.nn.softmax(s, axis=-1)
    o = jnp.einsum('bhsm,bmhd->bshd', p.astype(v.dtype), v).reshape(B, S, X_HEADS * X_HEAD_DIM)
    return o @ w_o

def swiglu(x, w_gu, w_d):
    g, u = jnp.split(x @ w_gu, 2, axis=-1)
    return (jax.nn.silu(g) * u) @ w_d

def moe_swiglu(x, w_router, b_router, w_gu, w_d):
    B, S, D = x.shape
    xt = x.reshape(B * S, D)
    T = xt.shape[0]
    N = T * TOP_K
    logits = (xt @ w_router).astype(jnp.float32) + b_router.astype(jnp.float32)
    top_logit, top_e = lax.top_k(logits, TOP_K)
    top_w = jax.nn.softmax(top_logit, axis=-1)
    flat_e = top_e.reshape(-1)
    flat_w = top_w.reshape(-1)
    order = jnp.argsort(flat_e)
    se = flat_e[order]
    stok = (order // TOP_K).astype(jnp.int32)
    sw = flat_w[order]
    counts = jnp.bincount(flat_e, length=N_EXPERTS)
    starts = jnp.cumsum(counts) - counts
    padded = (counts + MOE_BLOCK - 1) // MOE_BLOCK * MOE_BLOCK
    pad_end = jnp.cumsum(padded)
    pad_start = pad_end - padded
    dest = pad_start[se] + jnp.arange(N) - starts[se]
    n_rows = (N + N_EXPERTS * MOE_BLOCK + MOE_BLOCK - 1) // MOE_BLOCK * MOE_BLOCK
    row_tok = jnp.zeros((n_rows,), jnp.int32).at[dest].set(stok)
    row_w = jnp.zeros((n_rows,), x.dtype).at[dest].set(sw.astype(x.dtype))
    n_blk = n_rows // MOE_BLOCK
    blk_e = jnp.minimum(jnp.searchsorted(pad_end, jnp.arange(n_blk) * MOE_BLOCK, side='right'), N_EXPERTS - 1)
    xb = xt[row_tok].reshape(n_blk, MOE_BLOCK, D)

    def expert_block(args):
        xe, e = args
        g, u = jnp.split(xe @ w_gu[e], 2, axis=-1)
        return (jax.nn.silu(g) * u) @ w_d[e]

    yb = lax.map(expert_block, (xb, blk_e)).reshape(n_rows, D)
    out = jnp.zeros_like(xt).at[row_tok].add(yb * row_w[:, None])
    return out.reshape(B, S, D)

def setup_inputs(seed: int = 0) -> dict:
    key = jax.random.key(seed)
    ks = jax.random.split(key, 32)
    f32 = jnp.float32
    L = DEPTH
    beta = DEEPNORM_BETA

    def nrm(k, shape, scale):
        return jax.random.normal(k, shape, f32) * scale

    def gain(k, shape):
        return 1.0 + 0.01 * jax.random.normal(k, shape, f32)

    return {
        'x': nrm(ks[0], (BATCH, SEQ, D_MODEL), 1.0),
        'mem': nrm(ks[1], (BATCH, MEM_LEN, D_MODEL), 1.0),
        'w_in': nrm(ks[2], (L, D_MODEL, D_IN), D_MODEL ** -0.5),
        'b_merge': nrm(ks[3], (L, N_BRANCH, D_MODEL), 0.02),
        'attn_sink': nrm(ks[4], (L, SWA_HEADS), 1.0),
        'rel_bias': nrm(ks[5], (NUM_BUCKETS, SWA_HEADS), 0.2),
        'w_alpha2': nrm(ks[6], (L, GLA_GATE_RANK, GLA_HEADS * GLA_DK), GLA_GATE_RANK ** -0.5),
        'b_alpha2': nrm(ks[7], (L, GLA_HEADS * GLA_DK), 0.1),
        'gla_gain': gain(ks[8], (L, GLA_HEADS * GLA_DV)),
        'conv_w': nrm(ks[9], (L, CONV_K, CONV_CH), CONV_K ** -0.5),
        'w_branch': nrm(ks[10], (L, N_BRANCH, BRANCH_WIDTH, D_MODEL), BRANCH_WIDTH ** -0.5 * beta),
        'w_out': nrm(ks[11], (L, D_MODEL, D_MODEL), D_MODEL ** -0.5 * beta),
        'ln1_g': gain(ks[12], (L, D_MODEL)),
        'ln1_b': nrm(ks[13], (L, D_MODEL), 0.02),
        'w_xq': nrm(ks[14], (L, D_MODEL, X_HEADS * X_HEAD_DIM), D_MODEL ** -0.5),
        'w_xkv': nrm(ks[15], (L, D_MODEL, 2 * X_HEADS * X_HEAD_DIM), D_MODEL ** -0.5),
        'w_xo': nrm(ks[16], (L, X_HEADS * X_HEAD_DIM, D_MODEL), (X_HEADS * X_HEAD_DIM) ** -0.5 * beta),
        'ln2_g': gain(ks[17], (L, D_MODEL)),
        'ln2_b': nrm(ks[18], (L, D_MODEL), 0.02),
        'w_ff_gu': nrm(ks[19], (N_DENSE, D_MODEL, 2 * DENSE_FF), D_MODEL ** -0.5),
        'w_ff_d': nrm(ks[20], (N_DENSE, DENSE_FF, D_MODEL), DENSE_FF ** -0.5 * beta),
        'w_router': nrm(ks[21], (N_MOE, D_MODEL, N_EXPERTS), D_MODEL ** -0.5),
        'b_router': nrm(ks[22], (N_MOE, N_EXPERTS), 0.01),
        'w_e_gu': nrm(ks[23], (N_MOE, N_EXPERTS, D_MODEL, 2 * EXPERT_FF), D_MODEL ** -0.5),
        'w_e_d': nrm(ks[24], (N_MOE, N_EXPERTS, EXPERT_FF, D_MODEL), EXPERT_FF ** -0.5 * beta),
        'ln3_g': gain(ks[25], (L, D_MODEL)),
        'ln3_b': nrm(ks[26], (L, D_MODEL), 0.02),
    }

def reference(x, mem, w_in, b_merge, attn_sink, rel_bias, w_alpha2, b_alpha2, gla_gain, conv_w,
              w_branch, w_out, ln1_g, ln1_b, w_xq, w_xkv, w_xo, ln2_g, ln2_b,
              w_ff_gu, w_ff_d, w_router, b_router, w_e_gu, w_e_d, ln3_g, ln3_b):
    alpha = DEEPNORM_ALPHA
    pos_bias = rel_position_bias(rel_bias)
    for l in range(DEPTH):
        h = hybrid_mixer(x, w_in[l], b_merge[l], attn_sink[l], pos_bias, w_alpha2[l], b_alpha2[l],
                         gla_gain[l], conv_w[l], w_branch[l], w_out[l])
        x = layer_norm(alpha * x + h, ln1_g[l], ln1_b[l])
        h = cross_attention(x, mem, w_xq[l], w_xkv[l], w_xo[l])
        x = layer_norm(alpha * x + h, ln2_g[l], ln2_b[l])
        if l % 2 == 0:
            h = swiglu(x, w_ff_gu[l // 2], w_ff_d[l // 2])
        else:
            h = moe_swiglu(x, w_router[l // 2], b_router[l // 2], w_e_gu[l // 2], w_e_d[l // 2])
        x = layer_norm(alpha * x + h, ln3_g[l], ln3_b[l])
    return x


_drawn_inputs = setup_inputs


def setup_inputs(seed=0):
    import zlib

    import numpy as np

    out = dict(_drawn_inputs(seed))
    spreads = {}
    factors = {'b_merge': 8.0,
     'attn_sink': 8.0,
     'rel_bias': 8.0,
     'w_alpha2': 4.703,
     'b_alpha2': 8.0,
     'gla_gain': 27.459,
     'ln1_g': 3.365,
     'ln2_g': 2.931,
     'b_router': 4.974,
     'ln3_g': 3.429}
    for name, (base, spread) in spreads.items():
        noise = np.random.default_rng([zlib.crc32(name.encode()), seed]).standard_normal(out[name].shape)
        drawn = base * np.exp(spread * noise) if base else spread * noise
        out[name] = jnp.asarray(drawn.astype(out[name].dtype))
    for name, factor in factors.items():
        out[name] = (out[name] * factor).astype(out[name].dtype)
    return out
```

```python
from contextlib import ExitStack

import concourse.bass as bass
from concourse import mybir

F32 = mybir.dt.float32
F32R = mybir.dt.float32r
I32 = mybir.dt.int32
U32 = mybir.dt.uint32
ALU = mybir.AluOpType
ACT = mybir.ActivationFunctionType
AX = mybir.AxisListType

P = 128
DEPTH = 2
T = 256
TT = T // P
D = 1024
KD = D // P
CHUNK = 64
NC = T // CHUNK
BUCKETS = 32
SWA_HEADS = 8
PAIRS = 4
RANK = 16
BRANCH = 512
KB = BRANCH // P
FF = 2816
EXPERTS = 8
EFF = 3584
LN_EPS = 1e-5
ALPHA = float((2 * DEPTH) ** 0.25)
NEG = -1e30
REL = 192

UNIT = 2048
RAW = 6
SPLIT = 3

C_Q, C_K, C_V, C_BQ, C_BK, C_BV, C_BR, C_LR, C_CB, C_CC, C_CH, C_G = (
    0, 512, 640, 768, 1024, 1280, 1792, 2304, 2320, 2832, 3344, 3856)

GU_STEPS = EFF // 512
D_UNITS = EFF // 256
E_UNITS = 4 * GU_STEPS + D_UNITS
EK = EFF // P
OVER = 3
COLS = EXPERTS + OVER + 1


class Plan:

    def __init__(self):
        self.units = []
        self.unit_no = {}
        self.step_no = {}
        self.bank = {}
        self.before = {}
        self.used = [0] * 8
        self.steps = 0
        self.ring = {0: 0, 4: 0}

    def take(self, key, n, ring, banks=None):
        got = []
        for i in range(n):
            if banks is None:
                b = ring + self.ring[ring] % 4
                self.ring[ring] += 1
            else:
                b = banks[i]
            got.append((b, self.used[b]))
            self.used[b] += 1
        self.bank[key] = got

    def unit(self, key, floats=UNIT, n=1, ring=0, banks=None):
        self.unit_no[key] = len(self.units)
        self.units.append((key, floats))
        self.before[key] = len(self.units)
        if n:
            self.take(key, n, ring, banks)

    def step(self, key, n=1, ring=4, banks=None):
        self.step_no[key] = self.steps
        self.steps += 1
        self.before[key] = len(self.units)
        self.take(key, n, ring, banks)


def plan_dense():
    p = Plan()
    for i in range(4):
        p.step(("xT", 0, 0, i))
    for l in range(DEPTH):
        p.unit((l, "kv"), n=2)
        p.unit((l, "q", 0))
        p.unit((l, "q", 1))
        p.unit((l, "lr"), floats=KD * RANK)
        p.unit((l, "bk"))
        p.step((l, "lrT"))
        for c in range(NC):
            p.step((l, "scores", c))
        p.unit((l, "bv", 0))
        p.step((l, "z"))
        p.unit((l, "bv", 1))
        p.unit((l, "bq"))
        p.step((l, "cum"))
        p.step((l, "end"))
        p.unit((l, "br", 0))
        p.unit((l, "br", 1))
        for c in range(NC):
            p.step((l, "pT", c))
        for c in range(NC):
            p.step((l, "state", c))
        p.unit((l, "cc", 0))
        for c in range(NC):
            p.step((l, "pv", c))
        p.unit((l, "cc", 1))
        for t in range(TT):
            p.step((l, "gla", t))
        p.unit((l, "ch", 0))
        p.unit((l, "ch", 1))
        p.unit((l, "cb", 0))
        for i in range(2):
            p.step((l, "ybT", i))
        p.unit((l, "cb", 1))
        for half in range(2):
            for b in range(3):
                p.unit((l, "gate", half, b, 0))
                p.unit((l, "gate", half, b, 1))
                p.unit((l, "branch", half, b), n=2)
        for n in range(4):
            p.unit((l, "out", n))
            p.step((l, "memT", n))
        for n in range(4):
            p.unit((l, "xk", n))
        for n in range(4):
            p.unit((l, "xv", n))
        for i in range(4):
            p.step(("xT", l, 1, i))
        p.unit((l, "xq", 0))
        p.unit((l, "xq", 1))
        p.step((l, "xs", 0))
        p.unit((l, "xq", 2))
        p.step((l, "xs", 1))
        p.step((l, "xp", 0))
        p.unit((l, "xq", 3))
        p.step((l, "xs", 2))
        p.step((l, "xp", 1))
        p.step((l, "xo", 0))
        p.step((l, "xs", 3))
        p.step((l, "xp", 2))
        p.step((l, "xo", 1))
        p.step((l, "xp", 3))
        p.step((l, "xo", 2))
        p.step((l, "xo", 3))
        for n in range(4):
            p.unit((l, "xw", n))
        for i in range(4):
            p.step(("xT", l, 2, i))
        if l == 0:
            for n in range(FF // 256):
                p.unit((l, "fg", n))
                p.unit((l, "fu", n))
            for n in range(FF // 256):
                last = n == FF // 256 - 1
                p.unit((l, "fd", n), n=0)
                if n == 0:
                    p.take((l, "ffn"), 4, 4)
            p.unit_no[(l, "ffn")] = p.unit_no[(l, "fd", FF // 256 - 1)]
            p.before[(l, "ffn")] = len(p.units)
            for i in range(4):
                p.step(("xT", 1, 0, i))
    return p


def plan_expert(first):
    p = Plan()
    if not first:
        for j in range(GU_STEPS):
            b = 2 * (j % 2)
            p.unit(("g", j, 0), n=1, banks=[b])
            p.unit(("g", j, 1), n=0)
            p.unit(("u", j, 0), n=1, banks=[b + 1])
            p.unit(("u", j, 1), n=0)
            if j == 0:
                p.step("selT", banks=[4])
            else:
                p.step(("hT", j - 1), banks=[4 + j % 2])
        for n in range(D_UNITS):
            p.unit(("d", n), n=0)
            if n == 0:
                p.take("y", 2, 4, banks=[6, 7])
            if n == 1:
                p.step(("hT", GU_STEPS - 1), banks=[5])
            if n == 7:
                p.step("dispatch", 4, banks=[0, 1, 2, 3])
        p.unit_no["y"] = p.unit_no[("d", D_UNITS - 1)]
        p.before["y"] = len(p.units)
        for i in range(4):
            p.step(("combine", i), banks=[4 + i % 2])
    else:
        p.step("dispatch", 4, banks=[0, 1, 2, 3])
    return p


def hybrid_layers(nc, t, scratch, out):
    dense = plan_dense()
    route = Plan()
    route.used, route.steps = list(dense.used), dense.steps
    route.step("logits", banks=[4])
    route.step("ranks", banks=[5])
    route.step("dispatch", 4, banks=[0, 1, 2, 3])
    rnd = plan_expert(False)
    U0 = len(dense.units)
    S0 = route.steps

    ctx = ExitStack()
    with ctx:
        KIB = 1024
        base = (nc.sbuf_base + 63) // 64 * 64

        def at(name, shape, dt, off):
            return nc.alloc_sbuf_tensor_at(name, shape, dt, offset=base + int(off))

        def sem(name):
            return ctx.enter_context(nc.semaphore(name))

        raw = at("raw", [P, RAW, UNIT], F32, 0)
        w_hi = at("w_hi", [P, SPLIT, UNIT], F32R, 48 * KIB)
        w_lo = at("w_lo", [P, SPLIT, UNIT], F32R, 72 * KIB)
        x = at("x", [P, TT, D], F32, 96 * KIB)
        xT_hi = at("xT_hi", [P, KD, T], F32R, 104 * KIB)
        xT_lo = at("xT_lo", [P, KD, T], F32R, 112 * KIB)
        A0 = 120 * KIB
        y_hi = at("y_hi", [P, 3, KB, T], F32R, A0)
        y_lo = at("y_lo", [P, 3, KB, T], F32R, A0 + 12 * KIB)
        q_bd = at("q_bd", [P, PAIRS, NC, P], F32, A0 + 24 * KIB)
        prob = at("prob", [P, NC, PAIRS, P], F32, A0 + 32 * KIB)
        cc = at("cc", [P, KB, T], F32, A0 + 24 * KIB)
        cu = at("cu", [P, KB, T + 8], F32, A0 + 28 * KIB)
        cy = at("cy", [P, KB, T], F32, A0 + 33 * KIB)
        merged_hi = at("merged_hi", [P, KD, T], F32R, A0 + 24 * KIB)
        merged_lo = at("merged_lo", [P, KD, T], F32R, A0 + 32 * KIB)
        kT = at("kT", [P, T], F32, A0 + 40 * KIB)
        vwin = at("vwin", [P, 3, P], F32, A0 + 41 * KIB)
        probT = at("probT", [P, NC, PAIRS * P], F32, A0 + 42.5 * KIB)
        gates = at("gates", [P, 2, 4, T], F32, A0 + 40 * KIB)
        bk = at("bk", [P, TT, T], F32, A0 + 50.5 * KIB)
        kdec = at("kdec", [P, 2, TT, T], F32, A0 + 52.5 * KIB)
        bv = at("bv", [P, TT, BRANCH], F32, A0 + 56.5 * KIB)
        sq = at("sq", [P, TT, BRANCH], F32, A0 + 56.5 * KIB)
        log_a = at("log_a", [P, TT, T], F32, A0 + 60.5 * KIB)
        bqT = at("bqT", [P, 2, T], F32, A0 + 62.5 * KIB)
        state = at("state", [P, NC, 2, T], F32, A0 + 64.5 * KIB)
        br = at("br", [P, TT, BRANCH], F32, A0 + 48 * KIB + 24.5 * KIB)
        gla = at("gla", [P, TT, BRANCH], F32, A0 + 52.5 * KIB)
        msum = at("msum", [P, 4, T], F32, A0 + 64.5 * KIB)
        memT_hi = at("memT_hi", [P, KD, T], F32R, A0)
        memT_lo = at("memT_lo", [P, KD, T], F32R, A0 + 8 * KIB)
        mem_tok = at("mem_tok", [P, TT, D], F32, A0 + 16 * KIB)
        xkT = at("xkT", [P, KD, T], F32, A0 + 24 * KIB)
        xv = at("xv", [P, TT, D], F32, A0 + 32 * KIB)
        xqT = at("xqT", [P, KD, T], F32, A0 + 40 * KIB)
        xprob = at("xprob", [P, 4, TT, T], F32, A0 + 48 * KIB)
        xprobT = at("xprobT", [P, 4, TT, T], F32, A0 + 64 * KIB)
        xoT_hi = at("xoT_hi", [P, KD, T], F32R, A0)
        xoT_lo = at("xoT_lo", [P, KD, T], F32R, A0 + 8 * KIB)
        ln_gb = at("ln_gb", [P, 2, D], F32, A0 + 56 * KIB)
        NF = FF // P
        hT_hi = at("hT_hi", [P, NF, T], F32R, A0)
        hT_lo = at("hT_lo", [P, NF, T], F32R, A0 + 22 * KIB)
        fsilu = at("fsilu", [P, 2, 512], F32, A0 + 44 * KIB)
        fprod = at("fprod", [P, 2, 512], F32, A0 + 48 * KIB)
        xtok_hi = at("xtok_hi", [P, TT, D], F32R, A0)
        xtok_lo = at("xtok_lo", [P, TT, D], F32R, A0 + 8 * KIB)
        xe_hi = at("xe_hi", [P, KD, P], F32R, A0 + 16 * KIB)
        xe_lo = at("xe_lo", [P, KD, P], F32R, A0 + 20 * KIB)
        eT_hi = at("eT_hi", [P, EK, P], F32R, A0 + 24 * KIB)
        eT_lo = at("eT_lo", [P, EK, P], F32R, A0 + 38 * KIB)
        eh = at("eh", [P, 2, 512], F32, A0 + 52 * KIB)
        ye_hi = at("ye_hi", [P, D], F32R, A0 + 64 * KIB)
        ye_lo = at("ye_lo", [P, D], F32R, A0 + 68 * KIB)
        acc = at("acc", [P, TT, D], F32, 104 * KIB)
        esilu = at("esilu", [P, 2, 512], F32, 112 * KIB)
        sel = at("sel", [P, TT, P], F32R, 116 * KIB)
        selT = at("selT", [P, TT, P], F32R, 117 * KIB)
        off = [A0 + 76.5 * KIB]

        def small(name, shape, dt=F32):
            n = 1
            for s in shape[1:]:
                n *= s
            o = off[0]
            off[0] += (4 * n + 31) // 32 * 32
            return at(name, shape, dt, o)

        mats = small("mats", [P, 3, P])
        ident, later, earlier = (mats[:, i, :] for i in range(3))
        ones = small("ones", [P, P])
        ind = small("ind", [P, 4])
        bias = small("bias", [P, PAIRS, P])
        sink = small("sink", [P, DEPTH, PAIRS])
        w_conv = small("w_conv", [P, DEPTH, 3, KB])
        b_gate = small("b_gate", [P, DEPTH, 3 * KD])
        gain = small("gain", [P, BRANCH])
        alpha2 = small("alpha2", [P, DEPTH, T])
        w_rt = small("w_rt", [P, KD, EXPERTS])
        w_rt_hi = small("w_rt_hi", [P, KD, EXPERTS], F32R)
        w_rt_lo = small("w_rt_lo", [P, KD, EXPERTS], F32R)
        b_rt = small("b_rt", [P, EXPERTS])
        lr = small("lr", [P, TT, RANK])
        lrT = small("lrT", [P, T])
        mx = small("mx", [P, NC, PAIRS])
        rs = small("rs", [P, NC, PAIRS])
        sk = small("sk", [P, NC, PAIRS])
        dec = small("dec", [P, 2, NC])
        ms = small("ms", [P, TT, 4])
        stats = small("stats", [P, TT, 2, 6])
        mv = small("mv", [P, TT, 2])
        rstd = small("rstd", [P, TT])
        nmr = small("nmr", [P, TT])
        xmx = small("xmx", [P, 4, TT])
        xsum = small("xsum", [P, 4, TT])
        xrec = small("xrec", [P, 4, TT])
        lg = small("lg", [P, TT, EXPERTS])
        top = small("top", [P, TT, 8])
        topi = small("topi", [P, TT, 8], U32)
        topf = small("topf", [P, TT, 8])
        wts = small("wts", [P, TT, 2])
        ovf = small("ovf", [P, 4])
        ovi = small("ovi", [P, 4], I32)
        small_end, off[0] = off[0], 118.5 * KIB + 64
        pick = small("pick", [P, TT, EXPERTS])
        pick2 = small("pick2", [P, TT, EXPERTS])
        picked = small("picked", [P, TT, EXPERTS])
        pos = small("pos", [P, TT, COLS])
        wtab = small("wtab", [P, TT, COLS])
        cnt = small("cnt", [P, EXPERTS])
        ov = small("ov", [P, EXPERTS])
        rank = small("rank", [P, 2, EXPERTS])
        oneh = small("oneh", [P, OVER, EXPERTS])
        tmp8 = small("tmp8", [P, TT, EXPERTS])
        assert off[0] <= A0 and small_end <= nc.sbuf_usable_end - base
        onehot = at("onehot", [BUCKETS, REL], F32, A0)
        table = at("table", [BUCKETS, SWA_HEADS], F32, A0 + 1 * KIB)
        diag = at("diag", [SWA_HEADS, REL], F32, A0 + 2 * KIB)
        iota = at("iota", [P, P], F32, 118 * KIB)
        iota8 = at("iota8", [P, EXPERTS], F32, 118.5 * KIB)

        bank = [ctx.enter_context(nc.psum_tensor(f"bank{i}", [P, 512], F32)) for i in range(8)]

        raw_loaded = [sem(f"raw_loaded{i}") for i in range(RAW)]
        hi_ready = sem("hi_ready")
        lo_ready = sem("lo_ready")
        unit_done = sem("unit_done")
        step_done = sem("step_done")
        drained = [sem(f"drained{i}") for i in range(8)]
        x_loaded = sem("x_loaded")
        const_loaded = sem("const_loaded")
        bias_in = sem("bias_in")
        bias_mm = sem("bias_mm")
        bias_diag = sem("bias_diag")
        bias_out = sem("bias_out")
        bias_loaded = sem("bias_loaded")
        gain_loaded = sem("gain_loaded")
        zeroed = sem("zeroed")
        ln_loaded = sem("ln_loaded")
        mem_loaded = sem("mem_loaded")
        late_loaded = sem("late_loaded")
        dve_link = sem("dve_link")
        act_link = sem("act_link")
        pool_link = sem("pool_link")
        shifted = sem("shifted")
        expd = sem("expd")
        normed = sem("normed")
        log1p_ready = sem("log1p_ready")
        decay_ready = sem("decay_ready")
        kdec_ready = sem("kdec_ready")
        gla_ms = sem("gla_ms")
        gla_sqrt = sem("gla_sqrt")
        yb_ready = sem("yb_ready")
        state_ready = sem("state_ready")
        y_ready = sem("y_ready")
        gate_used = sem("gate_used")
        sum_ready = sem("sum_ready")
        var_ready = sem("var_ready")
        sqrt_ready = sem("sqrt_ready")
        scale_ready = sem("scale_ready")
        act_normed = sem("act_normed")
        ln_dve = sem("ln_dve")
        ln_pool = sem("ln_pool")
        xmax_ready = sem("xmax_ready")
        xexp_ready = sem("xexp_ready")
        xprob_ready = sem("xprob_ready")
        silu_ready = sem("silu_ready")
        h_ready = sem("h_ready")
        hT_hi_ready = sem("hT_hi_ready")
        hT_ready = sem("hT_ready")
        y_hi_ready = sem("y_hi_ready")
        ye_ready = sem("ye_ready")
        sel_ready = sem("sel_ready")
        exp_top = sem("exp_top")
        top_ready = sem("top_ready")
        router_ready = sem("router_ready")
        picked_ready = sem("picked_ready")
        routed = sem("routed")
        xtok_ready = sem("xtok_ready")
        out_sent = sem("out_sent")

        block = ctx.enter_context(nc.Block())

        def product(key):
            if key in dense.unit_no:
                return unit_done, dense.unit_no[key] + 1
            return step_done, dense.step_no[key] + 1

        def await_banks(pe, uses, start=None):
            for b, n in uses:
                if n:
                    pe.wait_ge(drained[b], n)

        def feature_tile(w, l, c0, n=256):
            return w[l, :, c0:c0 + n].rearrange("(k p) n -> p k n", p=P)

        def source(key):
            l, name = key[0], key[1]
            w_in = t["w_in"]
            if name == "kv":
                return feature_tile(w_in, l, C_K)
            if name == "lr":
                return feature_tile(w_in, l, C_LR, RANK)
            if name in ("bk", "bq"):
                return feature_tile(w_in, l, C_BK if name == "bk" else C_BQ)
            cols = {"bv": C_BV, "br": C_BR, "cc": C_CC, "ch": C_CH, "cb": C_CB}
            if name in cols:
                return feature_tile(w_in, l, cols[name] + 256 * key[2])
            if name == "gate":
                _, _, half, b, n = key
                return feature_tile(w_in, l, C_G + b * D + half * 512 + n * 256)
            if name == "branch":
                _, _, half, b = key
                w = t["w_branch"][l, b, :, half * 512:half * 512 + 512]
                if b:
                    return w.rearrange("(k p) n -> p k n", p=P)
                return w
            if name == "out":
                return feature_tile(t["w_out"], l, 256 * key[2])
            if name in ("xk", "xv"):
                return feature_tile(t["w_xkv"], l, 256 * key[2] + (D if name == "xv" else 0))
            if name == "xq":
                return feature_tile(t["w_xq"], l, 256 * key[2])
            if name == "xw":
                return feature_tile(t["w_xo"], l, 256 * key[2])
            if name == "fg":
                return feature_tile(t["w_ff_gu"], 0, 256 * key[2])
            if name == "fu":
                return feature_tile(t["w_ff_gu"], 0, FF + 256 * key[2])
            assert name == "fd"
            return t["w_ff_d"][0, 256 * key[2]:256 * key[2] + 256, :].rearrange("(k p) n -> p k n", p=P)

        raw_target = []
        total = [0] * RAW

        def transfers(key):
            return 4 if key[1] == "q" else 2 if key[1] == "branch" and key[3] == 0 else 1

        for i, (key, _) in enumerate(dense.units):
            total[i % RAW] += 16 * transfers(key)
            raw_target.append(total[i % RAW])
        raw_base = list(total)

        @block.sync
        def _(sp):
            sp.dma_start(x[:, :, :], t["x"].rearrange("o (t p) d -> p (o t) d", p=P)).then_inc(x_loaded, 16)
            for i, (key, floats) in enumerate(dense.units):
                slot = i % RAW
                if i >= RAW:
                    sp.wait_ge(lo_ready, i - RAW + 1)
                if key[1] == "q":
                    dst = raw[:, slot, :].rearrange("p (k h g d) -> p k h g d", k=KD, h=2, g=2)
                    for g in range(2):
                        for h in range(2):
                            head = 4 * g + 2 * key[2] + h
                            sp.dma_start(dst[:, :, h, g, :], feature_tile(t["w_in"], key[0], C_Q + CHUNK * head, CHUNK))\
                              .then_inc(raw_loaded[slot], 16)
                elif transfers(key) == 2:
                    src = source(key)
                    dst = raw[:, slot, :].rearrange("p (k n) -> p k n", k=KB)
                    for g in range(2):
                        sp.dma_start(dst[64 * g:64 * g + 64], src[256 * g:256 * g + 256].rearrange("(k p) n -> p k n", p=64))\
                          .then_inc(raw_loaded[slot], 16)
                else:
                    src = source(key)
                    dst = raw[:, slot, 0:floats].rearrange("p (k n) -> p k n", k=src.shape[1])
                    sp.dma_start(dst, src).then_inc(raw_loaded[slot], 16)

            def expert(r, e):
                for i, (key, _) in enumerate(rnd.units):
                    slot = (U0 + i) % RAW
                    sp.wait_ge(lo_ready, r * E_UNITS + (U0 + i - RAW + 1))
                    if key[0] == "d":
                        n = key[1]
                        src = t["w_e_d"][0, bass.ds(e, 1), 256 * n:256 * n + 256, :]
                        k = 2
                    else:
                        name, j, half = key
                        c0 = 512 * j + (EFF if name == "u" else 0)
                        src = t["w_e_gu"][0, bass.ds(e, 1), 512 * half:512 * half + 512, c0:c0 + 512]
                        k = 4
                    sp.dma_start(raw[:, slot, :].rearrange("p (k n) -> p k n", k=k),
                                 src.rearrange("o (k p) n -> p (o k) n", p=P)).then_inc(raw_loaded[slot], 16)

            with sp.Fori(0, EXPERTS) as e:
                expert(e, e)
            sp.wait_ge(routed, 1)
            over = sp.value_load(ovi[0:1, 0:1], min_val=0, max_val=OVER)
            with sp.If(over > 0):
                with sp.Fori(0, OVER) as m:
                    e = sp.value_load(ovi[0:1, bass.ds(m + 1, 1)], min_val=0, max_val=EXPERTS - 1)
                    expert(m + EXPERTS, e)
            for i in range(TT):
                sp.wait_ge(ln_dve if i == 0 else ln_pool, 3 * DEPTH)
                sp.dma_start(out[0, i * P:(i + 1) * P, :], x[:, i, :]).then_inc(out_sent, 16)
            sp.wait_ge(out_sent, 16 * TT)

        @block.gpsimd
        def _(pool):
            links = [0]

            def link(ins):
                links[0] += 1
                ins.then_inc(pool_link, 1)
                pool.wait_ge(pool_link, links[0])

            def load(dst, src, s=const_loaded):
                pool.dma_start(dst, src).then_inc(s, 16)

            load(mats[:, :, :], t["c_mats"].rearrange("i p n -> p i n"))
            load(ind[:, :], t["c_ind"])
            load(table[:, :], t["rel_bias"], bias_in)
            load(onehot[:, :], t["c_onehot"], bias_in)
            load(alpha2[0:RANK, :, :], t["w_alpha2"].rearrange("l r n -> r l n"))
            load(alpha2[RANK:RANK + 1, :, :], t["b_alpha2"].rearrange("(o l) n -> o l n", o=1))
            load(w_conv[:, :, :, :].rearrange("p l k c -> p (l k c)"),
                 t["conv_w"].rearrange("p l k c -> p (l k c)"))
            load(b_gate[:, :, :].rearrange("p l c -> p (l c)"), t["b_merge"].rearrange("p l c -> p (l c)"))
            load(w_rt[:, :, :], t["w_router"][0].rearrange("(k p) e -> p k e", p=P))
            load(b_rt[:, :], t["b_router"][0:1, :].to_broadcast((P, EXPERTS)))
            for g in range(2):
                for l in range(DEPTH):
                    load(sink[64 * g:64 * g + 64, l, :], t["attn_sink"][l:l + 1, 4 * g:4 * g + 4].to_broadcast((64, 4)))
            pool.memset(ones[:, :], 1.0).then_inc(zeroed, 1)
            pool.wait_ge(zeroed, 1)
            pool.wait_ge(bias_diag, 1)
            pool.dma_start(scratch.rearrange("(h i r) -> h i r", h=SWA_HEADS, i=CHUNK),
                           diag[:, :].unsqueeze(1).to_broadcast((SWA_HEADS, CHUNK, REL))).then_inc(bias_out, 16)
            pool.wait_ge(bias_out, 16)
            for g in range(2):
                src = bass.AP(scratch.tensor, scratch.offset + 4 * g * CHUNK * REL + CHUNK - 1,
                              [[REL - 1, CHUNK], [CHUNK * REL, PAIRS], [1, P]])
                load(bias[64 * g:64 * g + 64, :, :], src, bias_loaded)

            def zero_offdiagonal(l):
                if l:
                    pool.wait_ge(*product(("xT", 1, 0, 0)))
                else:
                    pool.wait_ge(bias_mm, 1)
                link(pool.memset(q_bd[0:64, :, :, 64:P].rearrange("p a b n -> p (a b) n"), 0.0))
                link(pool.memset(q_bd[64:P, :, :, 0:64].rearrange("p a b n -> p (a b) n"), 0.0))
                link(pool.memset(state[0:64, :, :, P:T].rearrange("p a b n -> p (a b) n"), 0.0))
                pool.memset(state[64:P, :, :, 0:P].rearrange("p a b n -> p (a b) n"), 0.0).then_inc(zeroed, 1)
                pool.wait_ge(zeroed, l + 2)

            def layer_norm(n, g, b, l, free):
                pool.wait_ge(*free)
                pool.dma_start(ln_gb[:, 0, :], g[l:l + 1, :].to_broadcast((P, D))).then_inc(ln_loaded, 16)
                pool.dma_start(ln_gb[:, 1, :], b[l:l + 1, :].to_broadcast((P, D))).then_inc(ln_loaded, 16)
                pool.wait_ge(ln_loaded, 32 * (n + 1))
                pool.wait_ge(act_normed, n + 1)
                link(pool.tensor_tensor(x[:, 1, :], x[:, 1, :], ln_gb[:, 0, :], ALU.mult))
                pool.tensor_tensor(x[:, 1, :], x[:, 1, :], ln_gb[:, 1, :], ALU.add).then_inc(ln_pool, 1)
                pool.wait_ge(ln_pool, n + 1)

            for l in range(DEPTH):
                if l:
                    pool.wait_ge(yb_ready, 1)
                load(gain[:, :], t["gla_gain"][l:l + 1, :].to_broadcast((P, BRANCH)), gain_loaded)
                zero_offdiagonal(l)
                pool.wait_ge(*product((l, "branch", 1, 2)))
                pool.dma_start(mem_tok[:, :, :], t["mem"].rearrange("o (t p) d -> p (o t) d", p=P))\
                    .then_inc(mem_loaded, 16)
                layer_norm(3 * l, t["ln1_g"], t["ln1_b"], l, product((l, "branch", 1, 2)))
                layer_norm(3 * l + 1, t["ln2_g"], t["ln2_b"], l, (ln_dve, 3 * l + 1))
                if l == 0:
                    layer_norm(2, t["ln3_g"], t["ln3_b"], l, (ln_dve, 2))
            pool.wait_ge(step_done, route.step_no["logits"] + 1)
            load(iota[:, :], t["c_iota"][0:1, :].to_broadcast((P, P)), late_loaded)
            load(iota8[:, :], t["c_iota"][0:1, 0:EXPERTS].to_broadcast((P, EXPERTS)), late_loaded)
            layer_norm(5, t["ln3_g"], t["ln3_b"], 1, (ln_dve, 5))

        @block.scalar
        def _(act):
            split = [0]
            links = [0]

            def link(ins):
                links[0] += 1
                ins.then_inc(act_link, 1)
                act.wait_ge(act_link, links[0])

            def round_until(n):
                for u in range(split[0], min(n, U0)):
                    act.wait_ge(raw_loaded[u % RAW], raw_target[u])
                    if u >= SPLIT:
                        act.wait_ge(unit_done, u - SPLIT + 1)
                    f = dense.units[u][1]
                    act.activation(w_hi[:, u % SPLIT, 0:f], raw[:, u % RAW, 0:f], ACT.Copy).then_inc(hi_ready, 1)
                split[0] = max(split[0], n)

            def ready(key):
                round_until(dense.before[key] + SPLIT)
                act.wait_ge(*product(key))

            def done(ins, key, i=0):
                ins.then_inc(drained[dense.bank[key][i][0]], 1)

            def pb(key, i=0):
                return bank[dense.bank[key][i][0]]

            def normalize(n):
                act.wait_ge(var_ready, n + 1)
                act.activation(rstd[:, :], nmr[:, :], ACT.Sqrt).then_inc(sqrt_ready, 1)
                act.wait_ge(scale_ready, n + 1)
                act.activation(x[:, 1, :], x[:, 1, :], ACT.Identity, scale=rstd[:, 1:2], bias=nmr[:, 1:2])\
                   .then_inc(act_normed, 1)

            for l in range(DEPTH):
                ready((l, "kv"))
                if l == 0:
                    act.wait_ge(bias_mm, 1)
                done(act.activation(vwin[:, :, :], pb((l, "kv"), 1)[:, 0:3 * P], ACT.Copy), (l, "kv"), 1)
                act.wait_ge(zeroed, l + 2)
                for n in range(2):
                    ready((l, "q", n))
                    src = pb((l, "q", n))[:, :].rearrange("p (t c i) -> p t c i", t=2, c=NC)
                    act.activation(q_bd[0:64, 2 * n:2 * n + 2, :, 0:64], src[0:64], ACT.Copy, scale=CHUNK ** -0.5)
                    done(act.activation(q_bd[64:P, 2 * n:2 * n + 2, :, 64:P], src[64:P], ACT.Copy,
                                        scale=CHUNK ** -0.5), (l, "q", n))
                ready((l, "bv", 0))
                done(act.activation(bv[:, :, 0:256], pb((l, "bv", 0))[:, :], ACT.Copy), (l, "bv", 0))
                ready((l, "z"))
                link(act.activation(kdec[:, 0, :, :], pb((l, "z"))[:, :], ACT.Abs))
                link(act.activation(kdec[:, 0, :, :], kdec[:, 0, :, :], ACT.Exp, scale=-1.0))
                act.activation(log_a[:, :, :], kdec[:, 0, :, :], ACT.Ln, bias=1.0).then_inc(log1p_ready, 1)
                ready((l, "bv", 1))
                done(act.activation(bv[:, :, 256:512], pb((l, "bv", 1))[:, :], ACT.Copy), (l, "bv", 1))
                ready((l, "bq"))
                done(act.activation(bqT[:, :, :], pb((l, "bq"))[:, :], ACT.Copy, scale=CHUNK ** -0.5), (l, "bq"))
                act.wait_ge(shifted, l + 1)
                act.activation(prob[:, :, :, :], prob[:, :, :, :], ACT.Exp)
                act.activation(sk[:, :, :], sk[:, :, :], ACT.Exp).then_inc(expd, 1)
                ready((l, "cum"))
                done(act.activation(kdec[:, 0, :, :], pb((l, "cum"))[:, :], ACT.Exp), (l, "cum"))
                ready((l, "end"))
                act.activation(dec[:, :, :], pb((l, "end"))[:, 0:2 * NC], ACT.Exp).then_inc(decay_ready, 1)
                for n in range(2):
                    ready((l, "br", n))
                    done(act.activation(br[:, :, 256 * n:256 * n + 256], pb((l, "br", n))[:, :], ACT.Silu),
                         (l, "br", n))
                for c in range(NC):
                    ready((l, "pT", c))
                    done(act.activation(probT[:, c, :], pb((l, "pT", c))[:, :], ACT.Copy), (l, "pT", c))
                for n in range(2):
                    ready((l, "cc", n))
                    done(act.activation(cc[:, 2 * n:2 * n + 2, :], pb((l, "cc", n))[:, :], ACT.Copy), (l, "cc", n))
                for i in range(TT):
                    ready((l, "gla", i))
                    act.wait_ge(state_ready, l * NC + NC)
                    done(act.activation(gla[:, i, :], pb((l, "gla", i))[:, :], ACT.Copy), (l, "gla", i))
                act.wait_ge(gla_ms, l + 1)
                act.activation(ms[:, :, :], ms[:, :, :], ACT.Sqrt).then_inc(gla_sqrt, 1)
                for half in range(2):
                    for b in range(3):
                        n = (l * 2 + half) * 3 + b
                        if n % 6 >= 2 or l:
                            act.wait_ge(gate_used, n - 1)
                        for i in range(2):
                            key = (l, "gate", half, b, i)
                            ready(key)
                            for j in range(2):
                                tile = b * KD + 4 * half + 2 * i + j
                                ins = act.activation(gates[:, n % 2, 2 * i + j, :], pb(key)[:, T * j:T * j + T],
                                                     ACT.Sigmoid, bias=b_gate[:, l, tile:tile + 1])
                            done(ins, key)
                round_until(dense.before[(l, "memT", 3)] + SPLIT)
                for n in range(4):
                    ready((l, "xk", n))
                    done(act.activation(xkT[:, 2 * n:2 * n + 2, :], pb((l, "xk", n))[:, :], ACT.Copy), (l, "xk", n))
                    if n == 1:
                        normalize(3 * l)
                for n in range(4):
                    ready((l, "xv", n))
                    done(act.activation(xv[:, :, 256 * n:256 * n + 256], pb((l, "xv", n))[:, :], ACT.Copy), (l, "xv", n))

                def xattn_scores(h):
                    ready((l, "xs", h))
                    act.wait_ge(xmax_ready, 4 * l + h + 1)
                    src = pb((l, "xs", h))
                    act.activation(xprob[:, h, 0, :], src[:, 0:T], ACT.Exp, bias=xmx[:, h, 0:1],
                                   accum_out=xsum[:, h, 0:1])
                    act.activation(xprob[:, h, 1, :], src[:, T:2 * T], ACT.Exp, bias=xmx[:, h, 1:2],
                                   accum_out=xsum[:, h, 1:2]).then_inc(xexp_ready, 1)

                def xattn_probT(h):
                    ready((l, "xp", h))
                    done(act.activation(xprobT[:, h, :, :], pb((l, "xp", h))[:, :], ACT.Copy), (l, "xp", h))

                def xattn_q(n):
                    ready((l, "xq", n))
                    done(act.activation(xqT[:, 2 * n:2 * n + 2, :], pb((l, "xq", n))[:, :], ACT.Copy, scale=T ** -0.5),
                         (l, "xq", n))

                xattn_q(0)
                xattn_q(1)
                xattn_scores(0)
                xattn_q(2)
                xattn_scores(1)
                xattn_probT(0)
                xattn_q(3)
                xattn_scores(2)
                xattn_probT(1)
                xattn_scores(3)
                xattn_probT(2)
                xattn_probT(3)
                round_until(dense.before[(l, "xw", 3)] + SPLIT)
                normalize(3 * l + 1)
                if l == 0:
                    for n in range(FF // 256):
                        ready((l, "fg", n))
                        if n >= 2:
                            act.wait_ge(h_ready, n - 1)
                        done(act.activation(fsilu[:, n % 2, :], pb((l, "fg", n))[:, :], ACT.Silu)
                             , (l, "fg", n))
                    round_until(dense.before[(l, "ffn")] + SPLIT)
                    normalize(2)

            act.wait_ge(top_ready, 1)
            act.activation(wts[:, :, 1], wts[:, :, 1], ACT.Exp).then_inc(exp_top, 1)
            HF = FF // 256

            def x_hi(r, use0):
                for i in range(2):
                    act.wait_ge(step_done, r)
                    act.activation(xe_hi[:, 4 * i:4 * i + 4, :], bank[i][:, :], ACT.Copy).then_inc(drained[i], 1)

            def expert(r):
                done_to = [0]

                def round_to(n):
                    for i in range(done_to[0], min(n, E_UNITS)):
                        u = U0 + i
                        act.wait_ge(raw_loaded[u % RAW], r * (16 * E_UNITS // RAW) + (raw_base[u % RAW] + 16 * (i // RAW + 1)))
                        act.wait_ge(unit_done, r * E_UNITS + (u - SPLIT + 1))
                        act.activation(w_hi[:, u % SPLIT, :], raw[:, u % RAW, :], ACT.Copy).then_inc(hi_ready, 1)
                    done_to[0] = max(done_to[0], n)

                def wait_step(key):
                    act.wait_ge(step_done, r * rnd.steps + (S0 + rnd.step_no[key] + 1))

                for j in range(GU_STEPS):
                    n = rnd.unit_no[("g", j, 1)]
                    round_to(n + 1 + 2)
                    act.wait_ge(unit_done, r * E_UNITS + (U0 + n + 1))
                    b = 2 * (j % 2)
                    act.wait_ge(h_ready, r * GU_STEPS + (HF + j - 1))
                    act.activation(esilu[:, j % 2, :], bank[b][:, :], ACT.Silu).then_inc(drained[b], 1)
                    n = rnd.before["selT"] if j == 0 else rnd.before[("hT", j - 1)]
                    round_to(n + 2)
                    if j == 0:
                        wait_step("selT")
                        act.activation(selT[:, :, :], bank[4][:, 0:T], ACT.Copy).then_inc(drained[4], 1)
                    else:
                        wait_step(("hT", j - 1))
                        act.activation(eT_hi[:, 4 * j - 4:4 * j, :], bank[4 + j % 2][:, :], ACT.Copy).then_inc(hT_hi_ready, 1)
                round_to(rnd.before[("hT", GU_STEPS - 1)] + 2)
                wait_step(("hT", GU_STEPS - 1))
                act.activation(eT_hi[:, EK - 4:EK, :], bank[5][:, :], ACT.Copy).then_inc(hT_hi_ready, 1)
                round_to(rnd.before["dispatch"] + 2)
                wait_step("dispatch")
                for i in range(2):
                    act.activation(xe_hi[:, 4 * i:4 * i + 4, :], bank[i][:, :], ACT.Copy).then_inc(drained[i], 1)
                round_to(E_UNITS)
                act.wait_ge(unit_done, r * E_UNITS + (U0 + E_UNITS))
                act.activation(ye_hi[:, 0:512], bank[6][:, :], ACT.Copy).then_inc(y_hi_ready, 1)
                act.activation(ye_hi[:, 512:D], bank[7][:, :], ACT.Copy).then_inc(y_hi_ready, 1)

            act.wait_ge(step_done, route.step_no["dispatch"] + 1)
            for i in range(2):
                act.activation(xe_hi[:, 4 * i:4 * i + 4, :], bank[i][:, :], ACT.Copy).then_inc(drained[i], 1)
            with act.Fori(0, EXPERTS) as e:
                expert(e)
            act.wait_ge(routed, 1)
            over = act.value_load(ovi[0:1, 0:1], min_val=0, max_val=OVER)
            with act.If(over > 0):
                with act.Fori(0, OVER) as m:
                    expert(m + EXPERTS)
            normalize(5)

        @block.vector
        def _(dve):
            split = [0]
            links = [0]

            def link(ins):
                links[0] += 1
                ins.then_inc(dve_link, 1)
                dve.wait_ge(dve_link, links[0])

            def rest_until(n):
                for u in range(split[0], min(n, U0)):
                    dve.wait_ge(hi_ready, u + 1)
                    f = dense.units[u][1]
                    dve.tensor_tensor(w_lo[:, u % SPLIT, 0:f], raw[:, u % RAW, 0:f],
                                      w_hi[:, u % SPLIT, 0:f].bitcast(F32), ALU.subtract).then_inc(lo_ready, 1)
                split[0] = max(split[0], n)

            def ready(key):
                rest_until(dense.before[key] + SPLIT)
                dve.wait_ge(*product(key))

            def done(ins, key, i=0):
                ins.then_inc(drained[dense.bank[key][i][0]], 1)

            def pb(key, i=0):
                return bank[dense.bank[key][i][0]]

            def split_to(hi, lo, src):
                link(dve.tensor_copy(hi, src))
                return dve.tensor_tensor(lo, src, hi.bitcast(F32), ALU.subtract)

            def feature_split(l, w):
                for i in range(4):
                    key = ("xT", l, w, i)
                    ready(key)
                    src = pb(key)[:, :].rearrange("p (k t) -> p k t", k=2)
                    done(split_to(xT_hi[:, 2 * i:2 * i + 2, :], xT_lo[:, 2 * i:2 * i + 2, :], src), key)

            def layer_norm(n, src):
                for i in range(TT):
                    for h in range(2):
                        link(dve.bn_stats(stats[:, i, h, :], src[:, i, 512 * h:512 * h + 512]))
                for i in range(TT):
                    link(dve.bn_aggr(mv[:, i, :], stats[:, i, :, :].rearrange("p a b -> p (a b)")))
                dve.tensor_scalar(nmr[:, :], mv[:, :, 1], LN_EPS, None, ALU.add).then_inc(var_ready, 1)
                dve.wait_ge(sqrt_ready, n + 1)
                link(dve.reciprocal(rstd[:, :], rstd[:, :]))
                dve.scalar_tensor_tensor(out=nmr[:, :], in0=mv[:, :, 0], scalar=-1.0, in1=rstd[:, :],
                                         op0=ALU.mult, op1=ALU.mult).then_inc(scale_ready, 1)
                link(dve.tensor_scalar(x[:, 0, :], src[:, 0, :], mv[:, 0, 0:1], rstd[:, 0:1], ALU.subtract, ALU.mult))
                dve.wait_ge(ln_loaded, 32 * (n + 1))
                link(dve.tensor_tensor(x[:, 0, :], x[:, 0, :], ln_gb[:, 0, :], ALU.mult))
                dve.tensor_tensor(x[:, 0, :], x[:, 0, :], ln_gb[:, 1, :], ALU.add).then_inc(ln_dve, 1)

            def add_residual(key, n):
                ready(key)
                dst = x[:, :, 256 * n:256 * n + 256]
                done(dve.scalar_tensor_tensor(out=dst, in0=dst, scalar=ALPHA,
                                              in1=pb(key)[:, :].rearrange("p (t n) -> p t n", t=TT),
                                              op0=ALU.mult, op1=ALU.add), key)

            link(dve.memset(lrT[0:32, :], 1.0))
            dve.wait_ge(bias_mm, 1)
            dve.tensor_copy(diag[:, :], bank[7][0:SWA_HEADS, 0:REL]).then_inc(bias_diag, 1)
            feature_split(0, 0)
            dve.wait_ge(const_loaded, 16 * 12)
            dve.wait_ge(zeroed, 1)
            link(dve.tensor_copy(w_rt_hi[:, :, :], w_rt[:, :, :]))
            dve.tensor_tensor(w_rt_lo[:, :, :], w_rt[:, :, :], w_rt_hi[:, :, :].bitcast(F32), ALU.subtract)\
               .then_inc(router_ready, 1)

            for l in range(DEPTH):
                key = (l, "kv")
                ready(key)
                done(dve.tensor_copy(kT[:, :], pb(key)[:, 0:T]), key)
                key = (l, "lr")
                ready(key)
                done(dve.tensor_copy(lr[:, :, :], pb(key)[:, 0:TT * RANK].rearrange("p (t r) -> p t r", t=TT)), key)
                key = (l, "bk")
                ready(key)
                done(dve.tensor_copy(bk[:, :, :], pb(key)[:, :].rearrange("p (t n) -> p t n", t=TT)), key)
                key = (l, "lrT")
                ready(key)
                done(dve.tensor_copy(lrT[0:RANK, :], pb(key)[0:RANK, 0:T]), key)
                dve.wait_ge(bias_loaded, 32)
                for c in range(NC):
                    key = (l, "scores", c)
                    ready(key)
                    src = pb(key)[:, :].rearrange("p (t j) -> p t j", t=PAIRS)
                    if c:
                        done(dve.tensor_tensor(prob[:, c, :, :], src, bias[:, :, :], ALU.add), key)
                    else:
                        dve.tensor_tensor(prob[:, 0, :, 0:64], src[:, :, 0:64], bias[:, :, 64:P], ALU.add)
                        done(dve.tensor_scalar(prob[:, 0, :, 64:P], src[:, :, 64:P], 0.0, NEG, ALU.mult, ALU.add), key)
                b, n = dense.bank[(l, "scores", NC - 1)][0]
                dve.wait_ge(drained[b], n + 1)
                link(dve.tensor_reduce(mx[:, :, :], prob[:, :, :, :], AX.X, ALU.max))
                sink_b = sink[:, l:l + 1, :].to_broadcast((P, NC, PAIRS))
                link(dve.tensor_tensor(mx[:, :, :], mx[:, :, :], sink_b, ALU.max))
                dve.tensor_tensor(sk[:, :, :], sink_b, mx[:, :, :], ALU.subtract)
                dve.tensor_tensor(prob[:, :, :, :].rearrange("p c t j -> p (c t) j"),
                                  prob[:, :, :, :].rearrange("p c t j -> p (c t) j"),
                                  mx[:, :, :].rearrange("p c t -> p (c t)").unsqueeze(2).to_broadcast((P, NC * PAIRS, P)),
                                  ALU.subtract).then_inc(shifted, 1)
                key = (l, "z")
                ready(key)
                dve.wait_ge(log1p_ready, l + 1)
                done(dve.scalar_tensor_tensor(out=log_a[:, :, :], in0=pb(key)[:, :].rearrange("p (t n) -> p t n", t=TT),
                                              scalar=0.0, in1=log_a[:, :, :], op0=ALU.min, op1=ALU.subtract), key)
                rest_until(dense.before[(l, "bq")] + SPLIT)
                dve.wait_ge(expd, l + 1)
                link(dve.tensor_reduce(rs[:, :, :], prob[:, :, :, :], AX.X, ALU.add))
                link(dve.tensor_tensor(rs[:, :, :], rs[:, :, :], sk[:, :, :], ALU.add))
                link(dve.reciprocal(rs[:, :, :], rs[:, :, :]))
                dve.tensor_tensor(prob[:, :, :, :].rearrange("p c t j -> p (c t) j"),
                                  prob[:, :, :, :].rearrange("p c t j -> p (c t) j"),
                                  rs[:, :, :].rearrange("p c t -> p (c t)").unsqueeze(2).to_broadcast((P, NC * PAIRS, P)),
                                  ALU.mult).then_inc(normed, 1)
                key = (l, "end")
                ready(key)
                dve.wait_ge(decay_ready, l + 1)
                dve.sem_inc(drained[dense.bank[key][0][0]], 1)
                dve.scalar_tensor_tensor(out=kdec[:, 1, :, :], in0=bk[:, :, :], scalar=ind[:, 3:4],
                                         in1=kdec[:, 0, :, :], op0=ALU.mult, op1=ALU.mult).then_inc(kdec_ready, 1)
                dve.wait_ge(kdec_ready, 2 * l + 1)
                dve.scalar_tensor_tensor(out=kdec[:, 0, :, :], in0=bk[:, :, :], scalar=ind[:, 2:3],
                                         in1=kdec[:, 0, :, :], op0=ALU.mult, op1=ALU.mult).then_inc(kdec_ready, 1)
                dve.wait_ge(zeroed, l + 2)
                for c in range(NC):
                    key = (l, "state", c)
                    ready(key)
                    if c == 0:
                        dve.wait_ge(decay_ready, l + 1)
                    else:
                        dve.wait_ge(state_ready, l * NC + c)
                    for p2 in range(2):
                        for g in range(2):
                            rows, cols = slice(64 * g, 64 * g + 64), slice(P * g, P * g + P)
                            src = pb(key)[rows, T * p2 + P * g:T * p2 + P * g + P]
                            if c == 0:
                                ins = dve.tensor_copy(state[rows, 0, p2, cols], src)
                            else:
                                ins = dve.scalar_tensor_tensor(out=state[rows, c, p2, cols],
                                                               in0=state[rows, c - 1, p2, cols],
                                                               scalar=dec[rows, p2, c:c + 1], in1=src,
                                                               op0=ALU.mult, op1=ALU.add)
                    ins.then_inc(state_ready, 1)
                    dve.wait_ge(state_ready, l * NC + c + 1)
                    dve.sem_inc(drained[dense.bank[key][0][0]], 1)
                for c in range(NC):
                    key = (l, "pv", c)
                    ready(key)
                    src = pb(key)[:, :].rearrange("p (t n) -> p t n", t=PAIRS)
                    toks = slice(CHUNK * c, CHUNK * c + CHUNK)
                    dve.tensor_copy(y_hi[0:64, 0, :, toks], src[0:64, :, 0:64])
                    link(dve.tensor_copy(y_hi[64:P, 0, :, toks], src[64:P, :, 64:P]))
                    dve.tensor_tensor(y_lo[0:64, 0, :, toks], src[0:64, :, 0:64],
                                      y_hi[0:64, 0, :, toks].bitcast(F32), ALU.subtract)
                    done(dve.tensor_tensor(y_lo[64:P, 0, :, toks], src[64:P, :, 64:P],
                                           y_hi[64:P, 0, :, toks].bitcast(F32), ALU.subtract), key)
                rest_until(dense.before[(l, "gla", 1)] + SPLIT)
                for i in range(TT):
                    b, n = dense.bank[(l, "gla", i)][0]
                    dve.wait_ge(drained[b], n + 1)
                link(dve.tensor_tensor(sq[:, :, :], gla[:, :, :], gla[:, :, :], ALU.mult))
                link(dve.tensor_reduce(ms[:, :, :], sq[:, :, :].rearrange("p t (h v) -> p t h v", h=4), AX.X, ALU.add))
                dve.tensor_scalar(ms[:, :, :], ms[:, :, :], 1.0 / P, LN_EPS, ALU.mult, ALU.add).then_inc(gla_ms, 1)
                dve.wait_ge(gain_loaded, 16 * (l + 1))
                b, n = dense.bank[(l, "br", 1)][0]
                dve.wait_ge(drained[b], n + 1)
                dve.tensor_tensor(br[:, :, :], br[:, :, :], gain[:, :].unsqueeze(1).to_broadcast((P, TT, BRANCH)), ALU.mult)\
                   .then_inc(dve_link, 1)
                links[0] += 1
                dve.wait_ge(gla_sqrt, l + 1)
                link(dve.reciprocal(ms[:, :, :], ms[:, :, :]))
                link(dve.tensor_tensor(gla[:, :, :].rearrange("p t (h v) -> p (t h) v", h=4),
                                       gla[:, :, :].rearrange("p t (h v) -> p (t h) v", h=4),
                                       ms[:, :, :].rearrange("p t h -> p (t h)").unsqueeze(2).to_broadcast((P, TT * 4, P)),
                                       ALU.mult))
                dve.tensor_tensor(gla[:, :, :], gla[:, :, :], br[:, :, :], ALU.mult).then_inc(yb_ready, 1)
                for n in range(2):
                    key = (l, "cc", n)
                    b, m = dense.bank[key][0]
                    rest_until(dense.before[(l, "ch", n)] + SPLIT)
                    dve.wait_ge(drained[b], m + 1)
                    if n == 0:
                        link(dve.memset(cu[:, :, 0:2], 0.0))
                    key = (l, "ch", n)
                    ready(key)
                    done(dve.tensor_tensor(cu[:, 2 * n:2 * n + 2, 2:2 + T], pb(key)[:, :].rearrange("p (c t) -> p c t", c=2),
                                           cc[:, 2 * n:2 * n + 2, :], ALU.mult), key)
                b, n = dense.bank[(l, "ch", 1)][0]
                dve.wait_ge(drained[b], n + 1)
                for k in range(3):
                    for c in range(KB):
                        w = w_conv[:, l, k, c:c + 1]
                        src = cu[:, c, k:k + T]
                        if k == 0:
                            ins = dve.tensor_scalar(cy[:, c, :], src, w, None, ALU.mult)
                        else:
                            ins = dve.scalar_tensor_tensor(out=cy[:, c, :], in0=src, scalar=w, in1=cy[:, c, :],
                                                           op0=ALU.mult, op1=ALU.add)
                    link(ins)
                for n in range(2):
                    if n == 0:
                        key = (l, "cb", 0)
                        ready(key)
                        done(dve.tensor_tensor(cy[:, 0:2, :], pb(key)[:, :].rearrange("p (c t) -> p c t", c=2), cy[:, 0:2, :],
                                               ALU.mult), key)
                for i in range(2):
                    key = (l, "ybT", i)
                    ready(key)
                    done(split_to(y_hi[:, 1, 2 * i:2 * i + 2, :], y_lo[:, 1, 2 * i:2 * i + 2, :],
                                  pb(key)[:, :].rearrange("p (k t) -> p k t", k=2)), key)
                key = (l, "cb", 1)
                ready(key)
                done(dve.tensor_tensor(cy[:, 2:4, :], pb(key)[:, :].rearrange("p (c t) -> p c t", c=2), cy[:, 2:4, :],
                                       ALU.mult), key)
                b, n = dense.bank[key][0]
                dve.wait_ge(drained[b], n + 1)
                split_to(y_hi[:, 2, :, :], y_lo[:, 2, :, :], cy[:, :, :]).then_inc(y_ready, 1)
                dve.wait_ge(y_ready, 3 * l + 1)
                for half in range(2):
                    for br_no in range(3):
                        n = (l * 2 + half) * 3 + br_no
                        key = (l, "branch", half, br_no)
                        for i in range(2):
                            b, m = dense.bank[(l, "gate", half, br_no, i)][0]
                            rest_until(dense.before[(l, "gate", half, br_no, i)] + SPLIT)
                            dve.wait_ge(drained[b], m + 1)
                        ready(key)
                        if br_no == 0:
                            for i in range(2):
                                done(dve.tensor_tensor(msum[:, 2 * i:2 * i + 2, :],
                                                       pb(key, i)[:, :].rearrange("p (c t) -> p c t", c=2),
                                                       gates[:, n % 2, 2 * i:2 * i + 2, :], ALU.mult), key, i)
                            for i in range(2):
                                b, m = dense.bank[key][i]
                                dve.wait_ge(drained[b], m + 1)
                            dve.sem_inc(gate_used, 1)
                            continue
                        g = gates[:, n % 2, :, :]
                        for i in range(2):
                            gi = gates[:, n % 2, 2 * i:2 * i + 2, :]
                            done(dve.tensor_tensor(gi, pb(key, i)[:, :].rearrange("p (c t) -> p c t", c=2), gi, ALU.mult),
                                 key, i)
                        for i in range(2):
                            b, m = dense.bank[key][i]
                            dve.wait_ge(drained[b], m + 1)
                        dve.tensor_tensor(msum[:, :, :], msum[:, :, :], g, ALU.add).then_inc(gate_used, 1)
                        dve.wait_ge(gate_used, n + 1)
                    split_to(merged_hi[:, 4 * half:4 * half + 4, :], merged_lo[:, 4 * half:4 * half + 4, :], msum[:, :, :])\
                        .then_inc(y_ready, 1)
                    dve.wait_ge(y_ready, 3 * l + 2 + half)
                for n in range(4):
                    add_residual((l, "out", n), n)
                    key = (l, "memT", n)
                    ready(key)
                    done(split_to(memT_hi[:, 2 * n:2 * n + 2, :], memT_lo[:, 2 * n:2 * n + 2, :],
                                  pb(key)[:, :].rearrange("p (k t) -> p k t", k=2)), key)
                rest_until(dense.before[(l, "xk", 1)] + SPLIT)
                b, n = dense.bank[(l, "out", 3)][0]
                dve.wait_ge(drained[b], n + 1)
                layer_norm(3 * l, x)
                rest_until(dense.before[(l, "xv", 3)] + SPLIT)
                feature_split(l, 1)

                def xattn_max(h):
                    key = (l, "xs", h)
                    ready(key)
                    dve.tensor_reduce(xmx[:, h, :], pb(key)[:, :].rearrange("p (t m) -> p t m", t=TT), AX.X, ALU.max,
                                      negate=True).then_inc(xmax_ready, 1)

                def xattn_prob(h):
                    dve.wait_ge(xexp_ready, 4 * l + h + 1)
                    link(dve.reciprocal(xrec[:, h, :], xsum[:, h, :]))
                    dve.sem_inc(drained[dense.bank[(l, "xs", h)][0][0]], 1)
                    for i in range(TT):
                        ins = dve.tensor_scalar(xprob[:, h, i, :], xprob[:, h, i, :], xrec[:, h, i:i + 1], None, ALU.mult)
                    ins.then_inc(xprob_ready, 1)

                def xattn_out(h):
                    key = (l, "xo", h)
                    ready(key)
                    done(split_to(xoT_hi[:, 2 * h:2 * h + 2, :], xoT_lo[:, 2 * h:2 * h + 2, :],
                                  pb(key)[:, :].rearrange("p (k t) -> p k t", k=2)), key)

                xattn_max(0)
                xattn_prob(0)
                xattn_max(1)
                xattn_prob(1)
                xattn_max(2)
                xattn_prob(2)
                xattn_out(0)
                xattn_max(3)
                xattn_prob(3)
                for h in range(1, 4):
                    xattn_out(h)
                for n in range(4):
                    add_residual((l, "xw", n), n)
                b, n = dense.bank[(l, "xw", 3)][0]
                dve.wait_ge(drained[b], n + 1)
                rest_until(dense.before[("xT", l, 2, 3)] + SPLIT)
                layer_norm(3 * l + 1, x)
                feature_split(l, 2)
                if l:
                    continue
                for n in range(FF // 256):
                    b, m = dense.bank[(l, "fg", n)][0]
                    key = (l, "fu", n)
                    ready(key)
                    dve.wait_ge(drained[b], m + 1)
                    done(dve.tensor_tensor(fprod[:, n % 2, :], pb(key)[:, :], fsilu[:, n % 2, :], ALU.mult), key)
                    b, m = dense.bank[key][0]
                    dve.wait_ge(drained[b], m + 1)
                    src = fprod[:, n % 2, :].rearrange("p (k t) -> p k t", k=2)
                    split_to(hT_hi[:, 2 * n:2 * n + 2, :], hT_lo[:, 2 * n:2 * n + 2, :], src).then_inc(h_ready, 1)
                    dve.wait_ge(h_ready, n + 1)
                key = (l, "ffn")
                ready(key)
                for i in range(TT):
                    for h in range(2):
                        dst = x[:, i, 512 * h:512 * h + 512]
                        done(dve.scalar_tensor_tensor(out=dst, in0=dst, scalar=ALPHA, in1=pb(key, 2 * i + h)[:, :],
                                                      op0=ALU.mult, op1=ALU.add), key, 2 * i + h)
                for b, n in dense.bank[key]:
                    dve.wait_ge(drained[b], n + 1)
                layer_norm(2, x)
                feature_split(1, 0)

            dve.wait_ge(ln_pool, 3 * DEPTH - 1)
            split_to(xtok_hi[:, :, :], xtok_lo[:, :, :], x[:, :, :]).then_inc(xtok_ready, 1)
            dve.wait_ge(step_done, route.step_no["logits"] + 1)
            dve.tensor_tensor(lg[:, :, :], bank[4][:, 0:TT * EXPERTS].rearrange("p (t e) -> p t e", t=TT),
                              b_rt[:, :].unsqueeze(1).to_broadcast((P, TT, EXPERTS)), ALU.add).then_inc(drained[4], 1)
            dve.wait_ge(drained[4], route.bank["logits"][0][1] + 1)
            for i in range(TT):
                link(dve.max(top[:, i, :], lg[:, i, :]))
                link(dve.max_index(topi[:, i, :], top[:, i, :], lg[:, i, :]))
            link(dve.tensor_copy(topf[:, :, :], topi[:, :, :]))
            dve.tensor_tensor(wts[:, :, 1], top[:, :, 1], top[:, :, 0], ALU.subtract).then_inc(top_ready, 1)
            dve.wait_ge(exp_top, 1)
            link(dve.tensor_scalar(wts[:, :, 0], wts[:, :, 1], 1.0, None, ALU.add))
            link(dve.reciprocal(wts[:, :, 0], wts[:, :, 0]))
            link(dve.tensor_tensor(wts[:, :, 1], wts[:, :, 1], wts[:, :, 0], ALU.mult))
            link(dve.memset(wtab[:, :, :], 0.0))
            link(dve.memset(pos[:, :, :], -1.0))
            dve.wait_ge(late_loaded, 32)
            for i in range(TT):
                dve.tensor_scalar(pick[:, i, :], iota8[:, :], topf[:, i, 0:1], None, ALU.is_equal)
                link(dve.tensor_scalar(pick2[:, i, :], iota8[:, :], topf[:, i, 1:2], None, ALU.is_equal))
                link(dve.tensor_scalar(wtab[:, i, 0:EXPERTS], pick[:, i, :], wts[:, i, 0:1], None, ALU.mult))
                link(dve.scalar_tensor_tensor(out=wtab[:, i, 0:EXPERTS], in0=pick2[:, i, :], scalar=wts[:, i, 1:2],
                                              in1=wtab[:, i, 0:EXPERTS], op0=ALU.mult, op1=ALU.add))
            dve.tensor_tensor(picked[:, :, :], pick[:, :, :], pick2[:, :, :], ALU.add).then_inc(picked_ready, 1)
            dve.wait_ge(step_done, route.step_no["ranks"] + 1)
            dve.wait_ge(picked_ready, 1)
            rk = bank[5]
            link(dve.scalar_tensor_tensor(out=tmp8[:, :, :], in0=rk[:, 0:TT * EXPERTS].rearrange("p (t e) -> p t e", t=TT),
                                          scalar=1.0, in1=picked[:, :, :], op0=ALU.add, op1=ALU.mult))
            link(dve.tensor_scalar(pos[:, :, 0:EXPERTS], tmp8[:, :, :], -1.0, None, ALU.add))
            dve.tensor_copy(cnt[:, :], rk[:, TT * EXPERTS:TT * EXPERTS + EXPERTS]).then_inc(drained[5], 1)
            dve.wait_ge(drained[5], route.bank["ranks"][0][1] + 1)

            def make_sel(col):
                dve.tensor_scalar(sel[:, 0, :], iota[:, :], pos[:, 0, bass.ds(col, 1)], None, ALU.is_equal)
                dve.tensor_scalar(sel[:, 1, :], iota[:, :], pos[:, 1, bass.ds(col, 1)], None, ALU.is_equal)\
                   .then_inc(sel_ready, 1)

            make_sel(0)
            link(dve.tensor_scalar(ov[:, :], cnt[:, :], float(P), None, ALU.is_gt))
            link(dve.memset(rank[:, :, :], 0.0))
            link(dve.tensor_copy(rank[:, 0, 1:EXPERTS], ov[:, 0:EXPERTS - 1]))
            for i, d in enumerate((1, 2, 4)):
                a, b = i % 2, (i + 1) % 2
                link(dve.tensor_copy(rank[:, b, 0:d], rank[:, a, 0:d]))
                link(dve.tensor_tensor(rank[:, b, d:EXPERTS], rank[:, a, d:EXPERTS], rank[:, a, 0:EXPERTS - d], ALU.add))
            link(dve.tensor_reduce(ovf[:, 0:1], ov[:, :], AX.X, ALU.add))
            for m in range(OVER):
                link(dve.scalar_tensor_tensor(out=oneh[:, m, :], in0=rank[:, 1, :], scalar=float(m), in1=ov[:, :],
                                              op0=ALU.is_equal, op1=ALU.mult))
                link(dve.tensor_tensor(cnt[:, :], oneh[:, m, :], iota8[:, :], ALU.mult))
                link(dve.tensor_reduce(ovf[:, m + 1:m + 2], cnt[:, :], AX.X, ALU.add))
                ohb = oneh[:, m:m + 1, :].to_broadcast((P, TT, EXPERTS))
                link(dve.tensor_tensor(tmp8[:, :, :], pos[:, :, 0:EXPERTS], ohb, ALU.mult))
                link(dve.tensor_reduce(pos[:, :, EXPERTS + m], tmp8[:, :, :], AX.X, ALU.add))
                link(dve.tensor_scalar(pos[:, :, EXPERTS + m], pos[:, :, EXPERTS + m], float(-P), None, ALU.add))
                link(dve.tensor_tensor(tmp8[:, :, :], wtab[:, :, 0:EXPERTS], ohb, ALU.mult))
                link(dve.tensor_reduce(wtab[:, :, EXPERTS + m], tmp8[:, :, :], AX.X, ALU.add))
            dve.tensor_copy(ovi[:, :], ovf[:, :]).then_inc(routed, 1)
            dve.wait_ge(routed, 1)
            dve.wait_ge(step_done, route.step_no["logits"] + 1)
            link(dve.tensor_scalar(acc[:, :, :], x[:, :, :], ALPHA, None, ALU.mult))
            HF = FF // 256

            def expert(r):
                done_to = [0]

                def rest_to(n):
                    for i in range(done_to[0], min(n, E_UNITS)):
                        u = U0 + i
                        dve.wait_ge(hi_ready, r * E_UNITS + (u + 1))
                        dve.tensor_tensor(w_lo[:, u % SPLIT, :], raw[:, u % RAW, :], w_hi[:, u % SPLIT, :].bitcast(F32),
                                          ALU.subtract).then_inc(lo_ready, 1)
                    done_to[0] = max(done_to[0], n)

                def hidden_rest(j):
                    dve.wait_ge(hT_hi_ready, r * GU_STEPS + (j + 1))
                    b = 4 + (j + 1) % 2
                    dve.tensor_tensor(eT_lo[:, 4 * j:4 * j + 4, :], bank[b][:, :].rearrange("p (k s) -> p k s", k=4),
                                      eT_hi[:, 4 * j:4 * j + 4, :].bitcast(F32), ALU.subtract).then_inc(drained[b], 1)

                for j in range(GU_STEPS):
                    rest_to(rnd.unit_no[("u", j, 1)] + 1 + 2)
                    dve.wait_ge(unit_done, r * E_UNITS + (U0 + rnd.unit_no[("u", j, 1)] + 1))
                    b, n = rnd.bank[("g", j, 0)][0]
                    dve.wait_ge(drained[b], r * rnd.used[b] + (route.used[b] + n + 1))
                    dve.tensor_tensor(eh[:, j % 2, :], bank[b + 1][:, :], esilu[:, j % 2, :], ALU.mult)\
                       .then_inc(drained[b + 1], 1)
                    b, n = rnd.bank[("u", j, 0)][0]
                    dve.wait_ge(drained[b], r * rnd.used[b] + (route.used[b] + n + 1))
                    dve.sem_inc(h_ready, 1)
                    if j:
                        hidden_rest(j - 1)
                rest_to(rnd.before[("hT", GU_STEPS - 1)] + 2)
                hidden_rest(GU_STEPS - 1)
                make_sel(r + 1)
                rest_to(rnd.before["dispatch"] + 2)
                dve.wait_ge(step_done, r * rnd.steps + (S0 + rnd.step_no["dispatch"] + 1))
                for i in range(2):
                    dve.tensor_copy(xe_lo[:, 4 * i:4 * i + 4, :], bank[2 + i][:, :].rearrange("p (k s) -> p k s", k=4))\
                       .then_inc(drained[2 + i], 1)
                rest_to(E_UNITS)
                for i in range(2):
                    dve.wait_ge(y_hi_ready, r * 2 + (i + 1))
                    dve.tensor_tensor(ye_lo[:, 512 * i:512 * i + 512], bank[6 + i][:, :],
                                      ye_hi[:, 512 * i:512 * i + 512].bitcast(F32), ALU.subtract)\
                       .then_inc(drained[6 + i], 1)
                for i in range(4):
                    tile, half = i // 2, i % 2
                    b, n = rnd.bank[("combine", i)][0]
                    dve.wait_ge(step_done, r * rnd.steps + (S0 + rnd.step_no[("combine", i)] + 1))
                    dst = acc[:, tile, 512 * half:512 * half + 512]
                    dve.scalar_tensor_tensor(out=dst, in0=bank[b][:, :], scalar=wtab[:, tile, bass.ds(r, 1)], in1=dst,
                                             op0=ALU.mult, op1=ALU.add).then_inc(drained[b], 1)

            dve.wait_ge(step_done, route.step_no["dispatch"] + 1)
            for i in range(2):
                dve.tensor_copy(xe_lo[:, 4 * i:4 * i + 4, :], bank[2 + i][:, :].rearrange("p (k s) -> p k s", k=4))\
                   .then_inc(drained[2 + i], 1)
            with dve.Fori(0, EXPERTS) as e:
                expert(e)
            over = dve.value_load(ovi[0:1, 0:1], min_val=0, max_val=OVER)
            with dve.If(over > 0):
                with dve.Fori(0, OVER) as m:
                    expert(m + EXPERTS)
            dve.drain().then_inc(sum_ready, 1)
            dve.wait_ge(sum_ready, 1)
            link(dve.tensor_copy(x[:, :, :], acc[:, :, :]))
            layer_norm(5, x)

        @block.tensor
        def _(pe):
            def product3(dst, l_hi, l_lo, r_hi, r_lo, first, last):
                pe.matmul(dst, l_hi, r_hi, start=first, stop=False)
                pe.matmul(dst, l_hi, r_lo, start=False, stop=False)
                return pe.matmul(dst, l_lo, r_hi, start=False, stop=last)

            def weights(key):
                u = dense.unit_no[key]
                f = dense.units[u][1]
                return w_hi[:, u % SPLIT, 0:f], w_lo[:, u % SPLIT, 0:f]

            def begin(key):
                pe.wait_ge(lo_ready, dense.unit_no[key] + 1)
                if key in dense.bank:
                    await_banks(pe, dense.bank[key])
                hi, lo = weights(key)
                return hi, lo

            def pb(key, i=0):
                return bank[dense.bank[key][i][0]]

            def feature_form(key, a_hi, a_lo, kt=KD, tiles=2):
                hi, lo = begin(key)
                hi, lo = (w.rearrange("p (k n) -> p k n", k=kt) for w in (hi, lo))
                for n in range(tiles):
                    dst = pb(key, n // 2)[:, T * (n % 2):T * (n % 2) + T]
                    for k in range(kt):
                        wh, wl = hi[:, k, P * n:P * n + P], lo[:, k, P * n:P * n + P]
                        last = product3(dst, wh, wl, a_hi[:, k, :], a_lo[:, k, :], k == 0, k == kt - 1)
                last.then_inc(unit_done, 1)

            def token_form(key, a_hi, a_lo):
                hi, lo = (w.rearrange("p (k n) -> p k n", k=KD) for w in begin(key))
                cols = hi.shape[2]
                for i in range(TT):
                    dst = pb(key)[:, cols * i:cols * i + cols]
                    for k in range(KD):
                        toks = slice(P * i, P * i + P)
                        last = product3(dst, a_hi[:, k, toks], a_lo[:, k, toks], hi[:, k, :], lo[:, k, :],
                                        k == 0, k == KD - 1)
                last.then_inc(unit_done, 1)

            def begin_step(key):
                await_banks(pe, dense.bank[key])

            def after(key, i=0):
                b, n = dense.bank[key][i]
                pe.wait_ge(drained[b], n + 1)

            def transposes(key, src, k0):
                begin_step(key)
                for k in range(2):
                    for i in range(TT):
                        last = pe.transpose(pb(key)[:, T * k + P * i:T * k + P * i + P],
                                            src[:, i, P * (k0 + k):P * (k0 + k) + P], ident)
                last.then_inc(step_done, 1)

            def x_to_features(l, w):
                for i in range(4):
                    transposes(("xT", l, w, i), x, 2 * i)

            pe.wait_ge(bias_in, 32)
            pe.matmul(bank[7][0:SWA_HEADS, 0:REL], table[:, :], onehot[:, :], start=True, stop=True).then_inc(bias_mm, 1)
            pe.wait_ge(bias_diag, 1)
            pe.wait_ge(x_loaded, 16)
            pe.wait_ge(const_loaded, 16 * 12)
            x_to_features(0, 0)

            for l in range(DEPTH):
                for i in range(4):
                    after(("xT", l, 0, i))
                key = (l, "kv")
                hi, lo = (w.rearrange("p (k n) -> p k n", k=KD) for w in begin(key))
                for k in range(KD):
                    product3(pb(key)[:, 0:T], hi[:, k, 0:P], lo[:, k, 0:P], xT_hi[:, k, :], xT_lo[:, k, :],
                             k == 0, k == KD - 1)
                for w in range(3):
                    toks = slice(CHUNK * w, CHUNK * w + P)
                    for k in range(KD):
                        last = product3(pb(key, 1)[:, P * w:P * w + P], xT_hi[:, k, toks], xT_lo[:, k, toks],
                                        hi[:, k, P:2 * P], lo[:, k, P:2 * P], k == 0, k == KD - 1)
                last.then_inc(unit_done, 1)
                feature_form((l, "q", 0), xT_hi, xT_lo)
                feature_form((l, "q", 1), xT_hi, xT_lo)
                token_form((l, "lr"), xT_hi, xT_lo)
                token_form((l, "bk"), xT_hi, xT_lo)
                key = (l, "lrT")
                begin_step(key)
                after((l, "lr"))
                for i in range(TT):
                    last = pe.transpose(pb(key)[0:RANK, P * i:P * i + P], lr[:, i, :], ident)
                last.then_inc(step_done, 1)
                after((l, "kv"), 0)
                after((l, "q", 0))
                after((l, "q", 1))
                for c in range(NC):
                    key = (l, "scores", c)
                    begin_step(key)
                    k0 = CHUNK * max(c - 1, 0)
                    for i in range(PAIRS):
                        last = pe.matmul(pb(key)[:, P * i:P * i + P], q_bd[:, i, c, :], kT[:, k0:k0 + P], start=True, stop=True)
                    last.then_inc(step_done, 1)
                token_form((l, "bv", 0), xT_hi, xT_lo)
                key = (l, "z")
                begin_step(key)
                after((l, "lrT"))
                for i in range(TT):
                    dst = pb(key)[:, T * i:T * i + T]
                    last = pe.matmul(dst, lrT[0:RANK + 1, P * i:P * i + P], alpha2[0:RANK + 1, l, :], start=True, stop=True)
                last.then_inc(step_done, 1)
                token_form((l, "bv", 1), xT_hi, xT_lo)
                feature_form((l, "bq"), xT_hi, xT_lo)
                key = (l, "cum")
                begin_step(key)
                after((l, "z"))
                for i in range(TT):
                    last = pe.matmul(pb(key)[:, T * i:T * i + T], later, log_a[:, i, :], start=True, stop=True)
                last.then_inc(step_done, 1)
                key = (l, "end")
                begin_step(key)
                for p2 in range(2):
                    for i in range(TT):
                        c0 = NC * p2 + 2 * i
                        last = pe.matmul(pb(key)[:, c0:c0 + 2], log_a[:, i, P * p2:P * p2 + P], ind[:, 0:2],
                                         start=True, stop=True)
                last.then_inc(step_done, 1)
                token_form((l, "br", 0), xT_hi, xT_lo)
                token_form((l, "br", 1), xT_hi, xT_lo)
                pe.wait_ge(normed, l + 1)
                for c in range(NC):
                    key = (l, "pT", c)
                    begin_step(key)
                    for i in range(PAIRS):
                        last = pe.transpose(pb(key)[:, P * i:P * i + P], prob[:, c, i, :], ident)
                    last.then_inc(step_done, 1)
                pe.wait_ge(kdec_ready, 2 * l + 2)
                after((l, "bv", 0))
                after((l, "bv", 1))
                for c in range(NC):
                    key = (l, "state", c)
                    begin_step(key)
                    for p2 in range(2):
                        last = pe.matmul(pb(key)[:, T * p2:T * p2 + T], kdec[:, c % 2, c // 2, P * p2:P * p2 + P],
                                         bv[:, c // 2, T * p2:T * p2 + T], start=True, stop=True)
                    last.then_inc(step_done, 1)
                feature_form((l, "cc", 0), xT_hi, xT_lo)
                after((l, "kv"), 1)
                for c in range(NC):
                    key = (l, "pv", c)
                    begin_step(key)
                    after((l, "pT", c))
                    pe.matmul(pb(key)[:, :], vwin[:, max(c - 1, 0), :], probT[:, c, :], start=True, stop=True)\
                      .then_inc(step_done, 1)
                feature_form((l, "cc", 1), xT_hi, xT_lo)
                after((l, "bq"))
                pe.wait_ge(state_ready, NC * (l + 1))
                for i in range(TT):
                    key = (l, "gla", i)
                    begin_step(key)
                    for h in range(2):
                        c = 2 * i + h
                        for p2 in range(2):
                            last = pe.matmul(pb(key)[64 * h:64 * h + 64, T * p2:T * p2 + T],
                                             bqT[:, p2, CHUNK * c:CHUNK * c + CHUNK], state[:, c, p2, :],
                                             start=True, stop=True)
                    last.then_inc(step_done, 1)
                feature_form((l, "ch", 0), xT_hi, xT_lo)
                feature_form((l, "ch", 1), xT_hi, xT_lo)
                feature_form((l, "cb", 0), xT_hi, xT_lo)
                pe.wait_ge(yb_ready, l + 1)
                for i in range(2):
                    transposes((l, "ybT", i), gla, 2 * i)
                feature_form((l, "cb", 1), xT_hi, xT_lo)
                for half in range(2):
                    for b in range(3):
                        for i in range(2):
                            feature_form((l, "gate", half, b, i), xT_hi, xT_lo)
                        if half == 0 and b == 0:
                            after((l, "pv", NC - 1))
                        if half == 0 and b == 1:
                            after((l, "ybT", 0))
                            after((l, "ybT", 1))
                        if half == 0 and b == 2:
                            pe.wait_ge(y_ready, 3 * l + 1)
                        feature_form((l, "branch", half, b), y_hi[:, b], y_lo[:, b], kt=KB, tiles=4)
                pe.wait_ge(y_ready, 3 * l + 3)
                pe.wait_ge(mem_loaded, 16 * (l + 1))
                for n in range(4):
                    token_form((l, "out", n), merged_hi, merged_lo)
                    transposes((l, "memT", n), mem_tok, 2 * n)
                for n in range(4):
                    after((l, "memT", n))
                for n in range(4):
                    feature_form((l, "xk", n), memT_hi, memT_lo)
                for n in range(4):
                    token_form((l, "xv", n), memT_hi, memT_lo)
                pe.wait_ge(ln_dve, 3 * l + 1)
                pe.wait_ge(ln_pool, 3 * l + 1)
                x_to_features(l, 1)
                for i in range(4):
                    after(("xT", l, 1, i))

                def xattn_scores(h):
                    key = (l, "xs", h)
                    begin_step(key)
                    after((l, "xq", h))
                    after((l, "xk", h))
                    for i in range(TT):
                        for k in range(2):
                            last = pe.matmul(pb(key)[:, T * i:T * i + T], xqT[:, 2 * h + k, P * i:P * i + P],
                                             xkT[:, 2 * h + k, :], start=(k == 0), stop=(k == 1))
                    last.then_inc(step_done, 1)

                def xattn_probT(h):
                    key = (l, "xp", h)
                    begin_step(key)
                    pe.wait_ge(xprob_ready, 4 * l + h + 1)
                    for m in range(2):
                        for i in range(TT):
                            last = pe.transpose(pb(key)[:, T * m + P * i:T * m + P * i + P],
                                                xprob[:, h, i, P * m:P * m + P], ident)
                    last.then_inc(step_done, 1)

                def xattn_out(h):
                    key = (l, "xo", h)
                    begin_step(key)
                    after((l, "xp", h))
                    after((l, "xv", h))
                    for k in range(2):
                        for m in range(2):
                            last = pe.matmul(pb(key)[:, T * k:T * k + T], xv[:, m, 256 * h + P * k:256 * h + P * k + P],
                                             xprobT[:, h, m, :], start=(m == 0), stop=(m == 1))
                    last.then_inc(step_done, 1)

                feature_form((l, "xq", 0), xT_hi, xT_lo)
                feature_form((l, "xq", 1), xT_hi, xT_lo)
                xattn_scores(0)
                feature_form((l, "xq", 2), xT_hi, xT_lo)
                xattn_scores(1)
                xattn_probT(0)
                feature_form((l, "xq", 3), xT_hi, xT_lo)
                xattn_scores(2)
                xattn_probT(1)
                xattn_out(0)
                xattn_scores(3)
                xattn_probT(2)
                xattn_out(1)
                xattn_probT(3)
                xattn_out(2)
                xattn_out(3)
                for h in range(4):
                    after((l, "xo", h))
                for n in range(4):
                    token_form((l, "xw", n), xoT_hi, xoT_lo)
                pe.wait_ge(ln_dve, 3 * l + 2)
                pe.wait_ge(ln_pool, 3 * l + 2)
                x_to_features(l, 2)
                for i in range(4):
                    after(("xT", l, 2, i))
                if l:
                    continue
                for n in range(FF // 256):
                    feature_form((l, "fg", n), xT_hi, xT_lo)
                    feature_form((l, "fu", n), xT_hi, xT_lo)
                key = (l, "ffn")
                await_banks(pe, dense.bank[key])
                for n in range(FF // 256):
                    pe.wait_ge(h_ready, n + 1)
                    hi, lo = (w.rearrange("p (k n) -> p k n", k=2) for w in begin((l, "fd", n)))
                    for k in range(2):
                        kk = 2 * n + k
                        for i in range(TT):
                            toks = slice(P * i, P * i + P)
                            for h in range(2):
                                cols = slice(512 * h, 512 * h + 512)
                                last = product3(pb(key, 2 * i + h)[:, :], hT_hi[:, kk, toks], hT_lo[:, kk, toks],
                                                hi[:, k, cols], lo[:, k, cols], kk == 0, kk == NF - 1)
                    last.then_inc(unit_done, 1)
                pe.wait_ge(ln_dve, 3)
                pe.wait_ge(ln_pool, 3)
                x_to_features(1, 0)

            b, n = route.bank["logits"][0]
            pe.wait_ge(drained[b], n)
            pe.wait_ge(router_ready, 1)
            for i in range(TT):
                toks = slice(P * i, P * i + P)
                for k in range(KD):
                    last = product3(bank[b][:, EXPERTS * i:EXPERTS * i + EXPERTS], xT_hi[:, k, toks], xT_lo[:, k, toks],
                                    w_rt_hi[:, k, :], w_rt_lo[:, k, :], k == 0, k == KD - 1)
            last.then_inc(step_done, 1)
            b, n = route.bank["ranks"][0]
            pe.wait_ge(drained[b], n)
            pe.wait_ge(picked_ready, 1)
            E = EXPERTS
            pe.matmul(bank[b][:, 0:E], earlier, picked[:, 0, :], start=True, stop=True)
            pe.matmul(bank[b][:, E:2 * E], earlier, picked[:, 1, :], start=True, stop=False)
            pe.matmul(bank[b][:, E:2 * E], ones[:, :], picked[:, 0, :], start=False, stop=True)
            pe.matmul(bank[b][:, 2 * E:3 * E], ones[:, :], picked[:, 0, :], start=True, stop=False)
            pe.matmul(bank[b][:, 2 * E:3 * E], ones[:, :], picked[:, 1, :], start=False, stop=True).then_inc(step_done, 1)

            def dispatch():
                for part, src in enumerate((xtok_hi, xtok_lo)):
                    for k in range(KD):
                        dst = bank[2 * part + k // 4][:, P * (k % 4):P * (k % 4) + P]
                        for i in range(TT):
                            last = pe.matmul(dst, src[:, i, P * k:P * k + P], sel[:, i, :], start=(i == 0), stop=(i == TT - 1))
                last.then_inc(step_done, 1)

            for b, n in route.bank["dispatch"]:
                pe.wait_ge(drained[b], n)
            pe.wait_ge(xtok_ready, 1)
            pe.wait_ge(sel_ready, 1)
            dispatch()

            def expert(r):
                def drained_to(b, n):
                    pe.wait_ge(drained[b], r * rnd.used[b] + (route.used[b] + n))

                def unit(key):
                    i = rnd.unit_no[key]
                    pe.wait_ge(lo_ready, r * E_UNITS + (U0 + i + 1))
                    s = (U0 + i) % SPLIT
                    kt = 2 if key[0] == "d" else 4
                    return (w[:, s, :].rearrange("p (k n) -> p k n", k=kt) for w in (w_hi, w_lo))

                def columns(name, j):
                    b, n = rnd.bank[(name, j, 0)][0]
                    for half in range(2):
                        hi, lo = unit((name, j, half))
                        if half == 0:
                            drained_to(b, n)
                        for k in range(4):
                            kk = 4 * half + k
                            last = product3(bank[b][:, :], xe_hi[:, kk, :], xe_lo[:, kk, :], hi[:, k, :], lo[:, k, :],
                                            kk == 0, kk == KD - 1)
                        last.then_inc(unit_done, 1)

                def hidden_transposes(j):
                    b, n = rnd.bank[("hT", j)][0]
                    drained_to(b, n)
                    pe.wait_ge(h_ready, r * GU_STEPS + (FF // 256 + j + 1))
                    for k in range(4):
                        last = pe.transpose(bank[b][:, P * k:P * k + P], eh[:, j % 2, P * k:P * k + P], ident)
                    last.then_inc(step_done, 1)

                for i in range(4):
                    pe.wait_ge(drained[i], r * rnd.used[i] + route.used[i])
                for j in range(GU_STEPS):
                    columns("g", j)
                    columns("u", j)
                    if j:
                        hidden_transposes(j - 1)
                        continue
                    b, n = rnd.bank["selT"][0]
                    drained_to(b, n)
                    for i in range(TT):
                        last = pe.transpose(bank[b][:, P * i:P * i + P], sel[:, i, :].bitcast(F32), ident)
                    last.then_inc(step_done, 1)
                for n in range(D_UNITS):
                    hi, lo = unit(("d", n))
                    if n == 0:
                        for b, m in rnd.bank["y"]:
                            drained_to(b, m)
                    if n % 2 == 0:
                        b, m = rnd.bank[("hT", n // 2)][0]
                        drained_to(b, m + 1)
                    for k in range(2):
                        kk = 2 * n + k
                        for h in range(2):
                            cols = slice(512 * h, 512 * h + 512)
                            last = product3(bank[6 + h][:, :], eT_hi[:, kk, :], eT_lo[:, kk, :], hi[:, k, cols], lo[:, k, cols],
                                            kk == 0, kk == EK - 1)
                    last.then_inc(unit_done, 1)
                    if n == 1:
                        hidden_transposes(GU_STEPS - 1)
                    if n == 7:
                        for b, m in rnd.bank["dispatch"]:
                            drained_to(b, m)
                        pe.wait_ge(sel_ready, r + 2)
                        dispatch()
                for b, m in rnd.bank["y"]:
                    drained_to(b, m + 1)
                b, m = rnd.bank["selT"][0]
                drained_to(b, m + 1)
                for i in range(4):
                    tile, half = i // 2, i % 2
                    b, m = rnd.bank[("combine", i)][0]
                    drained_to(b, m)
                    cols = slice(512 * half, 512 * half + 512)
                    pe.matmul(bank[b][:, :], selT[:, tile, :], ye_hi[:, cols], start=True, stop=False)
                    pe.matmul(bank[b][:, :], selT[:, tile, :], ye_lo[:, cols], start=False, stop=True).then_inc(step_done, 1)

            with pe.Fori(0, EXPERTS) as e:
                expert(e)
            pe.wait_ge(routed, 1)
            over = pe.value_load(ovi[0:1, 0:1], min_val=0, max_val=OVER)
            with pe.If(over > 0):
                with pe.Fori(0, OVER) as m:
                    expert(m + EXPERTS)


def shape_constants():
    import numpy as np

    n = np.arange(P)
    same = n[:, None] // CHUNK == n[None, :] // CHUNK
    mats = np.stack([np.eye(P), (same & (n[:, None] > n[None, :])) / 16.0, n[:, None] < n[None, :]])
    ind = np.zeros((P, 4))
    for g in range(2):
        ind[CHUNK * g:CHUNK * g + CHUNK, g] = 1 / 16.0
        ind[CHUNK * g:CHUNK * g + CHUNK, 2 + g] = 1.0
    rel = np.arange(-(P - 1), CHUNK)
    half, exact = BUCKETS // 2, BUCKETS // 4
    a = np.abs(rel)
    large = exact + (np.log(np.maximum(a, 1) / exact) / np.log(128 / exact) * (half - exact)).astype(np.int32)
    bucket = (rel > 0) * half + np.where(a < exact, a, np.minimum(large, half - 1))
    onehot = np.zeros((BUCKETS, REL))
    onehot[bucket, np.arange(len(rel))] = 1.0
    return {"c_mats": mats.astype(np.float32), "c_ind": ind.astype(np.float32),
            "c_onehot": onehot.astype(np.float32), "c_iota": np.arange(P, dtype=np.float32)[None, :]}


_INS = ["x", "mem", "w_in", "b_merge", "attn_sink", "rel_bias", "w_alpha2", "b_alpha2", "gla_gain", "conv_w",
        "w_branch", "w_out", "ln1_g", "ln1_b", "w_xq", "w_xkv", "w_xo", "ln2_g", "ln2_b", "w_ff_gu", "w_ff_d",
        "w_router", "b_router", "w_e_gu", "w_e_d", "ln3_g", "ln3_b"]


def kernel(**inputs):
    import numpy as np
    import concourse.bacc as bacc
    from concourse.bass_utils import run_bass_kernel_spmd as run

    nc = bacc.Bacc("TRN2", target_bir_lowering=False, num_devices=1)
    arrays = {name: np.ascontiguousarray(inputs[name]) for name in _INS}
    arrays["conv_w"] = np.ascontiguousarray(arrays["conv_w"].reshape(DEPTH, 3, KB, P).transpose(3, 0, 1, 2))
    arrays["b_merge"] = np.ascontiguousarray(arrays["b_merge"].reshape(DEPTH, 3 * KD, P).transpose(2, 0, 1))
    arrays.update(shape_constants())
    t = {name: nc.dram_tensor(name, a.shape, mybir.dt.from_np(a.dtype), kind="ExternalInput").ap()
         for name, a in arrays.items()}
    scratch = nc.dram_tensor("bias_by_offset", (SWA_HEADS * CHUNK * REL,), F32).ap()
    out = nc.dram_tensor("out", (1, T, D), F32, kind="ExternalOutput").ap()
    hybrid_layers(nc, t, scratch, out)
    r = run(nc, [arrays], core_ids=[0])
    return r.results[0]["out"]
```

```python
from contextlib import ExitStack

import concourse.bass as bass
from concourse import mybir

F32 = mybir.dt.float32
F32R = mybir.dt.float32r
I32 = mybir.dt.int32
U32 = mybir.dt.uint32
ALU = mybir.AluOpType
ACT = mybir.ActivationFunctionType
AX = mybir.AxisListType

P = 128
DEPTH = 2
T = 256
TT = T // P
D = 1024
KD = D // P
CHUNK = 64
NC = T // CHUNK
BUCKETS = 32
SWA_HEADS = 8
PAIRS = 4
RANK = 16
BRANCH = 512
KB = BRANCH // P
FF = 2816
EXPERTS = 8
EFF = 3584
LN_EPS = 1e-5
ALPHA = float((2 * DEPTH) ** 0.25)
NEG = -1e30
REL = 192

UNIT = 2048
RAW = 6
POOL_PART = 640
E_RAW = RAW + 1
SPLIT = 3

C_Q, C_K, C_V, C_BQ, C_BK, C_BV, C_BR, C_LR, C_CB, C_CC, C_CH, C_G = (
    0, 512, 640, 768, 1024, 1280, 1792, 2304, 2320, 2832, 3344, 3856)

GU_STEPS = EFF // 512
D_UNITS = EFF // 256
E_UNITS = 4 * GU_STEPS + D_UNITS
EK = EFF // P
OVER = 3
COLS = EXPERTS + OVER + 1


class Plan:

    def __init__(self):
        self.units = []
        self.unit_no = {}
        self.step_no = {}
        self.bank = {}
        self.before = {}
        self.used = [0] * 8
        self.steps = 0
        self.ring = {0: 0, 4: 0}
        self.rounded = {}

    def take(self, key, n, ring, banks=None):
        got = []
        for i in range(n):
            if banks is None:
                b = ring + self.ring[ring] % 4
                self.ring[ring] += 1
            else:
                b = banks[i]
            got.append((b, self.used[b]))
            self.used[b] += 1
        self.bank[key] = got

    def unit(self, key, floats=UNIT, n=1, ring=0, banks=None):
        self.unit_no[key] = len(self.units)
        self.units.append((key, floats))
        self.before[key] = len(self.units)
        if n:
            self.take(key, n, ring, banks)

    def step(self, key, n=1, ring=4, banks=None, rounded=False):
        if rounded:
            self.rounded[key] = len(self.rounded) + 1
        self.step_no[key] = self.steps
        self.steps += 1
        self.before[key] = len(self.units)
        self.take(key, n, ring, banks)


def plan_dense():
    p = Plan()
    for i in range(4):
        p.step(("xT", 0, 0, i), rounded=True)
    p.step("bias")
    for l in range(DEPTH):
        p.unit((l, "kv"))
        p.unit((l, "bk"))
        p.step((l, "vT"))
        p.unit((l, "lr"), floats=KD * P)
        p.unit((l, "q", 0))
        p.unit((l, "q", 1))
        p.unit((l, "bv", 0))
        for c in range(NC):
            p.step((l, "scores", c))
        p.unit((l, "bv", 1))
        p.step((l, "z"))
        p.unit((l, "bq"))
        p.unit((l, "br", 0))
        p.step((l, "cum"))
        p.step((l, "end"))
        p.unit((l, "br", 1))
        for c in range(NC):
            p.step((l, "pT", c))
        p.unit((l, "cc", 0))
        for c in range(NC):
            p.step((l, "state", c))
        p.unit((l, "cc", 1))
        for c in range(NC):
            p.step((l, "pv", c))
        p.unit((l, "ch", 0))
        for t in range(TT):
            p.step((l, "gla", t))
        p.unit((l, "ch", 1))
        p.unit((l, "cb", 0))
        p.unit((l, "cb", 1))
        for i in range(2):
            p.step((l, "ybT", i))
        for half in range(2):
            for b in range(3):
                p.unit((l, "gate", half, b, 0))
                p.unit((l, "gate", half, b, 1))
                p.unit((l, "branch", half, b), n=2)
        for n in range(4):
            p.step((l, "memT", n), rounded=True)
        for n in range(4):
            p.unit((l, "out", n))
        for n in range(l, 4):
            p.unit((l, "xk", n))
        for i in range(4):
            p.step(("xT", l, 1, i), rounded=True)
        p.unit((l, "xv", 0))
        p.unit((l, "xv", 1))
        p.unit((l, "xq", 0))
        p.unit((l, "xq", 1))
        p.step((l, "xs", 0))
        p.unit((l, "xq", 2))
        p.step((l, "xs", 1))
        p.step((l, "xp", 0))
        p.unit((l, "xq", 3))
        p.step((l, "xs", 2))
        p.step((l, "xp", 1))
        p.step((l, "xo", 0))
        p.unit((l, "xv", 2))
        p.step((l, "xs", 3))
        p.step((l, "xp", 2))
        p.step((l, "xo", 1))
        p.unit((l, "xv", 3))
        p.step((l, "xp", 3))
        p.step((l, "xo", 2))
        p.step((l, "xo", 3))
        for n in range(4):
            p.unit((l, "xw", n))
        if l == 0:
            p.unit((1, "xk", 0))
        for i in range(4):
            p.step(("xT", l, 2, i), rounded=True)
        if l == 0:
            for n in range(FF // 256):
                p.unit((l, "fg", n))
                p.unit((l, "fu", n))
            for n in range(FF // 256):
                p.unit((l, "fd", n), n=0)
                if n == 0:
                    p.take((l, "ffn"), 4, 4)
            p.unit_no[(l, "ffn")] = p.unit_no[(l, "fd", FF // 256 - 1)]
            p.before[(l, "ffn")] = len(p.units)
            for i in range(4):
                p.step(("xT", 1, 0, i), rounded=True)
    return p


def plan_expert(first):
    p = Plan()
    for j in range(GU_STEPS):
        b = 2 * (j % 2)
        p.unit(("g", j, 0), n=1, banks=[b])
        p.unit(("g", j, 1), n=0)
        p.unit(("u", j, 0), n=1, banks=[b + 1])
        p.unit(("u", j, 1), n=0)
        if j == 0 and not first:
            for i in range(4):
                p.step(("combine", i), banks=[4 + i])
        if j:
            p.step(("hT", j - 1), banks=[4 + j % 2])
        if j == 1:
            p.step("selT", banks=[6])
    for n in range(D_UNITS):
        p.unit(("d", n), n=0)
        if n == 0:
            p.take("y", 2, 4, banks=[6, 7])
        if n == 1:
            p.step(("hT", GU_STEPS - 1), banks=[5])
        if n == 7:
            p.step("dispatch", 4, banks=[0, 1, 2, 3])
    return p


def rounds(prev, first, later, n):
    return n if prev is None else prev * later + (first + n)


def hybrid_layers(nc, t, scratch, out):
    dense = plan_dense()
    route = Plan()
    route.used, route.steps = list(dense.used), dense.steps
    route.step("logits", 2, banks=[4, 6])
    route.step("ranks", banks=[5])
    route.step("dispatch", 4, banks=[0, 1, 2, 3])
    route.step("counts", banks=[5])
    first, rnd = plan_expert(True), plan_expert(False)
    U0 = len(dense.units)
    S0 = route.steps

    ctx = ExitStack()
    with ctx:
        KIB = 1024
        base = (nc.sbuf_base + 63) // 64 * 64

        def at(name, shape, dt, off):
            return nc.alloc_sbuf_tensor_at(name, shape, dt, offset=base + int(off))

        def sem(name):
            return ctx.enter_context(nc.semaphore(name))

        raw = at("raw", [P, RAW, UNIT], F32, 0)
        w_hi = at("w_hi", [P, SPLIT, UNIT], F32R, 48 * KIB)
        w_lo = at("w_lo", [P, SPLIT, UNIT], F32R, 72 * KIB)
        x = at("x", [P, TT, D], F32, 96 * KIB)
        xT_hi = at("xT_hi", [P, KD, T], F32R, 104 * KIB)
        xT_lo = at("xT_lo", [P, KD, T], F32R, 112 * KIB)
        A0 = 120 * KIB
        y_hi = at("y_hi", [P, 3, KB, T], F32R, A0)
        y_lo = at("y_lo", [P, 3, KB, T], F32R, A0 + 12 * KIB)
        gain = at("gain", [P, BRANCH], F32, A0 + 20 * KIB)
        q_bd = at("q_bd", [P, PAIRS, NC, P], F32, A0 + 24 * KIB)
        prob = at("prob", [P, NC, PAIRS, P], F32, A0 + 32 * KIB)
        cc = at("cc", [P, KB, T], F32, A0 + 24 * KIB)
        cu = at("cu", [P, KB, T + 8], F32, A0 + 28 * KIB)
        cy = at("cy", [P, KB, T], F32, A0 + 33 * KIB)
        merged_hi = at("merged_hi", [P, KD, T], F32R, A0 + 24 * KIB)
        merged_lo = at("merged_lo", [P, KD, T], F32R, A0 + 32 * KIB)
        kT = at("kT", [P, T], F32, A0 + 40 * KIB)
        vT = at("vT", [P, T], F32, A0 + 72.5 * KIB)
        lrT = at("lrT", [P, T], F32, A0 + 73.5 * KIB)
        vwin = at("vwin", [P, 3, P], F32, A0 + 41 * KIB)
        probT = at("probT", [P, NC, PAIRS * P], F32, A0 + 42.5 * KIB)
        gates = at("gates", [P, 2, 4, T], F32, A0 + 40 * KIB)
        bk = at("bk", [P, TT, T], F32, A0 + 50.5 * KIB)
        kdec = at("kdec", [P, 2, TT, T], F32, A0 + 52.5 * KIB)
        bv = at("bv", [P, TT, BRANCH], F32, A0 + 56.5 * KIB)
        sq = at("sq", [P, TT, BRANCH], F32, A0 + 56.5 * KIB)
        log_a = at("log_a", [P, TT, T], F32, A0 + 60.5 * KIB)
        bqT = at("bqT", [P, 2, T], F32, A0 + 62.5 * KIB)
        state = at("state", [P, NC, 2, T], F32, A0 + 64.5 * KIB)
        br = at("br", [P, TT, BRANCH], F32, A0 + 48 * KIB + 24.5 * KIB)
        gla = at("gla", [P, TT, BRANCH], F32, A0 + 52.5 * KIB)
        msum = at("msum", [P, 4, T], F32, A0 + 64.5 * KIB)
        memT_hi = at("memT_hi", [P, KD, T], F32R, A0)
        memT_lo = at("memT_lo", [P, KD, T], F32R, A0 + 8 * KIB)
        mem_tok = at("mem_tok", [P, TT, D], F32, A0 + 48 * KIB)
        xkT = at("xkT", [P, KD, T], F32, A0 + 24 * KIB)
        xv = at("xv", [P, TT, D], F32, A0 + 32 * KIB)
        xqT = at("xqT", [P, KD, T], F32, A0 + 40 * KIB)
        xprob = at("xprob", [P, 4, TT, T], F32, A0 + 48 * KIB)
        xprobT = at("xprobT", [P, 4, TT, T], F32, A0 + 64 * KIB)
        xoT_hi = at("xoT_hi", [P, KD, T], F32R, A0 + 16 * KIB)
        xoT_lo = at("xoT_lo", [P, KD, T], F32R, A0 + 56 * KIB)
        xn = at("xn", [P, 4, 2, T], F32, A0 + 48 * KIB)
        ln_gb = at("ln_gb", [P, 2, D], F32, A0 + 56 * KIB)
        NF = FF // P
        hT_hi = at("hT_hi", [P, NF, T], F32R, A0)
        hT_lo = at("hT_lo", [P, NF, T], F32R, A0 + 22 * KIB)
        fsilu = at("fsilu", [P, 2, 512], F32, A0 + 44 * KIB)
        fprod = at("fprod", [P, 2, 512], F32, A0 + 48 * KIB)
        xtok_hi = at("xtok_hi", [P, TT, D], F32R, A0)
        xtok_lo = at("xtok_lo", [P, TT, D], F32R, A0 + 8 * KIB)
        xe_hi = at("xe_hi", [P, KD, P], F32R, A0 + 16 * KIB)
        xe_lo = at("xe_lo", [P, KD, P], F32R, A0 + 20 * KIB)
        eT_hi = at("eT_hi", [P, EK, P], F32R, A0 + 24 * KIB)
        eT_lo = at("eT_lo", [P, EK, P], F32R, A0 + 38 * KIB)
        eh = at("eh", [P, 2, 512], F32, A0 + 52 * KIB)
        raw_more = at("raw_more", [P, UNIT], F32, A0 + 56 * KIB)
        last_gb = at("last_gb", [P, 2, D], F32, A0)
        ye_hi = at("ye_hi", [P, D], F32R, A0 + 64 * KIB)
        ye_lo = at("ye_lo", [P, D], F32R, A0 + 68 * KIB)
        acc = at("acc", [P, TT, D], F32, 104 * KIB)
        esilu = at("esilu", [P, 2, 512], F32, 112 * KIB)
        sel = at("sel", [P, TT, P], F32R, 116 * KIB)
        selT = at("selT", [P, TT, P], F32R, 117 * KIB)
        off = [A0 + 76.5 * KIB]

        def small(name, shape, dt=F32):
            n = 1
            for s in shape[1:]:
                n *= s
            o = off[0]
            off[0] += (4 * n + 31) // 32 * 32
            return at(name, shape, dt, o)

        mats = small("mats", [P, 3, P])
        ident, later, earlier = (mats[:, i, :] for i in range(3))
        ones = small("ones", [P, P])
        ind = small("ind", [P, 4])
        bias = small("bias", [P, PAIRS, P])
        sink = small("sink", [P, DEPTH, PAIRS])
        w_conv = small("w_conv", [P, DEPTH, 3, KB])
        b_gate = small("b_gate", [P, DEPTH, 3 * KD])
        alpha2 = small("alpha2", [P, DEPTH, T])
        w_rt = small("w_rt", [P, KD, EXPERTS])
        w_rt2 = small("w_rt2", [P, KD, 2, EXPERTS], F32R)
        iota = small("iota", [P, P])
        iota8 = iota[:, 0:EXPERTS]
        b_rt = small("b_rt", [P, EXPERTS])
        xk_early = small("xk_early", [P, 2, T])
        mx = small("mx", [P, NC, PAIRS])
        rs = small("rs", [P, NC, PAIRS])
        sk = small("sk", [P, NC, PAIRS])
        dec = small("dec", [P, 2, NC])
        ms = small("ms", [P, TT, 4])
        ln_f = small("ln_f", [P, 2, 3 * DEPTH, KD])
        stats = small("stats", [P, TT, 4, 6])
        mv = small("mv", [P, TT, 2])
        rstd = small("rstd", [P, TT])
        nmr = small("nmr", [P, TT])
        xmx = small("xmx", [P, 4, TT])
        xsum = small("xsum", [P, 4, TT])
        xrec = small("xrec", [P, 4, TT])
        lg = small("lg", [P, TT, EXPERTS])
        top = small("top", [P, TT, 8])
        topi = small("topi", [P, TT, 8], U32)
        topf = small("topf", [P, TT, 8])
        wts = small("wts", [P, TT, 2])
        ovf = small("ovf", [P, 4])
        ovi = small("ovi", [P, 4], I32)
        small_end, off[0] = off[0], 118.5 * KIB + 64
        pick = small("pick", [P, TT, EXPERTS])
        pick2 = small("pick2", [P, TT, EXPERTS])
        picked = small("picked", [P, TT, EXPERTS])
        pos = small("pos", [P, TT, COLS])
        wtab = small("wtab", [P, TT, COLS])
        cnt = small("cnt", [P, EXPERTS])
        ov = small("ov", [P, EXPERTS])
        rank = small("rank", [P, 2, EXPERTS])
        oneh = small("oneh", [P, OVER, EXPERTS])
        tmp8 = small("tmp8", [P, TT, EXPERTS])
        assert off[0] <= A0 and small_end <= nc.sbuf_usable_end - base
        onehot = at("onehot", [BUCKETS, REL], F32, A0)
        table = at("table", [BUCKETS, SWA_HEADS], F32, A0 + 1 * KIB)
        diag = at("diag", [SWA_HEADS, REL], F32, A0 + 2 * KIB)
        bank = [ctx.enter_context(nc.psum_tensor(f"bank{i}", [P, 512], F32)) for i in range(8)]

        raw_loaded = [sem(f"raw_loaded{i}") for i in range(E_RAW)]
        hi_ready = sem("hi_ready")
        lo_ready = sem("lo_ready")
        unit_done = sem("unit_done")
        step_done = sem("step_done")
        drained = [sem(f"drained{i}") for i in range(8)]
        x_loaded = sem("x_loaded")
        const_loaded = sem("const_loaded")
        bias_in = sem("bias_in")
        mats_loaded = sem("mats_loaded")
        bias_diag = sem("bias_diag")
        bias_out = sem("bias_out")
        bias_loaded = sem("bias_loaded")
        gain_loaded = sem("gain_loaded")
        zeroed = sem("zeroed")
        ln_loaded = sem("ln_loaded")
        mem_loaded = sem("mem_loaded")
        acc_ready = sem("acc_ready")
        dve_link = sem("dve_link")
        act_link = sem("act_link")
        pool_link = sem("pool_link")
        shifted = sem("shifted")
        expd = sem("expd")
        normed = sem("normed")
        log1p_ready = sem("log1p_ready")
        decay_ready = sem("decay_ready")
        kdec_ready = sem("kdec_ready")
        gla_ms = sem("gla_ms")
        gla_sqrt = sem("gla_sqrt")
        yb_ready = sem("yb_ready")
        state_ready = sem("state_ready")
        y_ready = sem("y_ready")
        gate_used = sem("gate_used")
        sum_ready = sem("sum_ready")
        var_ready = sem("var_ready")
        sqrt_ready = sem("sqrt_ready")
        scale_ready = sem("scale_ready")
        act_normed = sem("act_normed")
        dve_normed = sem("dve_normed")
        rounded = sem("rounded")
        ffn_done = sem("ffn_done")
        merged_ready = sem("merged_ready")
        ln_dve = sem("ln_dve")
        ln_pool = sem("ln_pool")
        xmax_ready = sem("xmax_ready")
        xexp_ready = sem("xexp_ready")
        xprob_ready = sem("xprob_ready")
        h_ready = sem("h_ready")
        hT_hi_ready = sem("hT_hi_ready")
        y_hi_ready = sem("y_hi_ready")
        sel_ready = sem("sel_ready")
        exp_top = sem("exp_top")
        top_ready = sem("top_ready")
        router_ready = sem("router_ready")
        picked_ready = sem("picked_ready")
        routed = sem("routed")
        xtok_hi_ready = sem("xtok_hi_ready")
        xtok_ready = sem("xtok_ready")
        rounds_done = sem("rounds_done")
        last_y_hi = sem("last_y_hi")
        last_y = sem("last_y")
        acc_done = sem("acc_done")
        last_sum = sem("last_sum")
        out_sent = sem("out_sent")

        CONSTS = 16 * 13

        block = ctx.enter_context(nc.Block())

        def product(key):
            if key in dense.unit_no:
                return unit_done, dense.unit_no[key] + 1
            return step_done, dense.step_no[key] + 1

        def await_banks(pe, uses):
            for b, n in uses:
                if n:
                    pe.wait_ge(drained[b], n)

        def feature_tile(w, l, c0, n=256):
            return w[l, :, c0:c0 + n].rearrange("(k p) n -> p k n", p=P)

        def source(key):
            l, name = key[0], key[1]
            w_in = t["w_in"]
            if name == "kv":
                return feature_tile(w_in, l, C_K)
            if name == "lr":
                return feature_tile(w_in, l, C_LR, P)
            if name in ("bk", "bq"):
                return feature_tile(w_in, l, C_BK if name == "bk" else C_BQ)
            cols = {"bv": C_BV, "br": C_BR, "cc": C_CC, "ch": C_CH, "cb": C_CB}
            if name in cols:
                return feature_tile(w_in, l, cols[name] + 256 * key[2])
            if name == "gate":
                _, _, half, b, n = key
                return feature_tile(w_in, l, C_G + b * D + half * 512 + n * 256)
            if name == "branch":
                _, _, half, b = key
                w = t["w_branch"][l, b, :, half * 512:half * 512 + 512]
                if b:
                    return w.rearrange("(k p) n -> p k n", p=P)
                return w
            if name == "out":
                return feature_tile(t["w_out"], l, 256 * key[2])
            if name in ("xk", "xv"):
                return feature_tile(t["w_xkv"], l, 256 * key[2] + (D if name == "xv" else 0))
            if name == "xq":
                return feature_tile(t["w_xq"], l, 256 * key[2])
            if name == "xw":
                return feature_tile(t["w_xo"], l, 256 * key[2])
            if name == "fg":
                return feature_tile(t["w_ff_gu"], 0, 256 * key[2])
            if name == "fu":
                return feature_tile(t["w_ff_gu"], 0, FF + 256 * key[2])
            assert name == "fd"
            return t["w_ff_d"][0, 256 * key[2]:256 * key[2] + 256, :].rearrange("(k p) n -> p k n", p=P)

        raw_target = []
        total = [0] * RAW

        def transfers(key):
            return 4 if key[1] == "q" else 2 if key[1] == "branch" and key[3] == 0 else 1

        for i, (key, _) in enumerate(dense.units):
            total[i % RAW] += 16 * transfers(key)
            raw_target.append(total[i % RAW])
        raw_base = list(total) + [0]

        def expert_raw(i):
            slot = (U0 + i % E_RAW) % RAW if i % E_RAW < RAW else RAW
            return slot, raw[:, slot, :] if slot < RAW else raw_more[:, :]

        assert E_UNITS % E_RAW == 0

        @block.sync
        def _(sp):
            for i, (key, floats) in enumerate(dense.units):
                slot = i % RAW
                if i == 1:
                    sp.dma_start(x[:, :, :], t["x"].rearrange("o (t p) d -> p (o t) d", p=P)).then_inc(x_loaded, 16)
                if i >= RAW:
                    sp.wait_ge(lo_ready, i - RAW + 1)
                if key[1] == "q":
                    dst = raw[:, slot, :].rearrange("p (k h g d) -> p k h g d", k=KD, h=2, g=2)
                    for g in range(2):
                        for h in range(2):
                            head = 4 * g + 2 * key[2] + h
                            sp.dma_start(dst[:, :, h, g, :], feature_tile(t["w_in"], key[0], C_Q + CHUNK * head, CHUNK))\
                              .then_inc(raw_loaded[slot], 16)
                elif transfers(key) == 2:
                    src = source(key)
                    dst = raw[:, slot, :].rearrange("p (k n) -> p k n", k=KB)
                    for g in range(2):
                        sp.dma_start(dst[64 * g:64 * g + 64], src[256 * g:256 * g + 256].rearrange("(k p) n -> p k n", p=64))\
                          .then_inc(raw_loaded[slot], 16)
                else:
                    src = source(key)
                    dst = raw[:, slot, 0:floats].rearrange("p (k n) -> p k n", k=src.shape[1])
                    sp.dma_start(dst, src).then_inc(raw_loaded[slot], 16)

            def expert(prev, e):
                for i, (key, _) in enumerate(rnd.units):
                    slot, place = expert_raw(i)
                    if prev is None and i < RAW:
                        sp.wait_ge(lo_ready, U0 + i - RAW + 1)
                    elif prev is None and i == RAW:
                        sp.wait_ge(ln_dve, 1)
                        sp.wait_ge(ln_pool, 3 * DEPTH - 1)
                    else:
                        sp.wait_ge(lo_ready, rounds(prev, E_UNITS, E_UNITS, U0 + i - E_RAW + 1))
                    if key[0] == "d":
                        n = key[1]
                        src = t["w_e_d"][0, bass.ds(e, 1), 256 * n:256 * n + 256, :]
                        k = 2
                    else:
                        name, j, half = key
                        c0 = 512 * j + (EFF if name == "u" else 0)
                        src = t["w_e_gu"][0, bass.ds(e, 1), 512 * half:512 * half + 512, c0:c0 + 512]
                        k = 4
                    sp.dma_start(place.rearrange("p (k n) -> p k n", k=k),
                                 src.rearrange("o (k p) n -> p (o k) n", p=P)).then_inc(raw_loaded[slot], 16)

            expert(None, 0)
            with sp.Fori(0, EXPERTS - 1) as e:
                expert(e, e + 1)
            sp.wait_ge(routed, 1)
            over = sp.value_load(ovi[0:1, 0:1], min_val=0, max_val=OVER)
            with sp.If(over > 0):
                with sp.Fori(0, OVER) as m:
                    e = sp.value_load(ovi[0:1, bass.ds(m + 1, 1)], min_val=0, max_val=EXPERTS - 1)
                    expert(m + (EXPERTS - 1), e)
            for i in range(TT):
                sp.wait_ge(ln_dve, 2 + i)
                if i:
                    sp.wait_ge(ln_pool, 3 * DEPTH)
                sp.dma_start(out[0, i * P:(i + 1) * P, :], x[:, i, :]).then_inc(out_sent, 16)
            sp.wait_ge(out_sent, 16 * TT)

        @block.gpsimd
        def _(pool):
            links = [0]

            def link(ins):
                links[0] += 1
                ins.then_inc(pool_link, 1)
                pool.wait_ge(pool_link, links[0])

            def load(dst, src, s=const_loaded):
                pool.dma_start(dst, src).then_inc(s, 16)

            def zero_offdiagonal(l):
                if l:
                    pool.wait_ge(*product(("xT", 1, 0, 0)))
                link(pool.memset(q_bd[0:64, :, :, 64:P].rearrange("p a b n -> p (a b) n"), 0.0))
                link(pool.memset(q_bd[64:P, :, :, 0:64].rearrange("p a b n -> p (a b) n"), 0.0))
                link(pool.memset(state[0:64, :, :, P:T].rearrange("p a b n -> p (a b) n"), 0.0))
                pool.memset(state[64:P, :, :, 0:P].rearrange("p a b n -> p (a b) n"), 0.0).then_inc(zeroed, 1)
                pool.wait_ge(zeroed, l + 2)

            load(onehot[:, :], t["c_onehot"], bias_in)
            load(table[:, :], t["rel_bias"], bias_in)
            pool.memset(ones[:, :], 1.0).then_inc(zeroed, 1)
            pool.wait_ge(zeroed, 1)
            zero_offdiagonal(0)
            pool.wait_ge(bias_diag, 1)
            pool.dma_start(scratch.rearrange("(h i r) -> h i r", h=SWA_HEADS, i=CHUNK),
                           diag[:, :].unsqueeze(1).to_broadcast((SWA_HEADS, CHUNK, REL))).then_inc(bias_out, 16)
            load(ind[:, :], t["c_ind"])
            load(ln_f[:, :, :, :].rearrange("p a n k -> p (a n k)"), t["ln_f"].rearrange("p a n k -> p (a n k)"))
            load(alpha2[0:RANK, :, :], t["w_alpha2"].rearrange("l r n -> r l n"))
            load(alpha2[RANK:RANK + 1, :, :], t["b_alpha2"].rearrange("(o l) n -> o l n", o=1))
            load(w_conv[:, :, :, :].rearrange("p l k c -> p (l k c)"),
                 t["conv_w"].rearrange("p l k c -> p (l k c)"))
            load(b_gate[:, :, :].rearrange("p l c -> p (l c)"), t["b_merge"].rearrange("p l c -> p (l c)"))
            pool.wait_ge(bias_out, 16)
            for g in range(2):
                src = bass.AP(scratch.tensor, scratch.offset + 4 * g * CHUNK * REL + CHUNK - 1,
                              [[REL - 1, CHUNK], [CHUNK * REL, PAIRS], [1, P]])
                load(bias[64 * g:64 * g + 64, :, :], src, bias_loaded)

            load(w_rt[:, :, :], t["w_router"][0].rearrange("(k p) e -> p k e", p=P))
            load(iota[:, :], t["c_iota"][0:1, :].to_broadcast((P, P)))
            load(b_rt[:, :], t["b_router"][0:1, :].to_broadcast((P, EXPERTS)))
            for g in range(2):
                for l in range(DEPTH):
                    load(sink[64 * g:64 * g + 64, l, :], t["attn_sink"][l:l + 1, 4 * g:4 * g + 4].to_broadcast((64, 4)))
            def load_gains(n, dst=ln_gb):
                l, w = divmod(n, 3)
                for i, v in enumerate((f"ln{w + 1}_g", f"ln{w + 1}_b")):
                    pool.dma_start(dst[:, i, :], t[v][l:l + 1, :].to_broadcast((P, D))).then_inc(ln_loaded, 16)

            def gain_and_bias(i):
                link(pool.tensor_tensor(x[:, i, :], x[:, i, :], ln_gb[:, 0, :], ALU.mult))
                return pool.tensor_tensor(x[:, i, :], x[:, i, :], ln_gb[:, 1, :], ALU.add)

            def layer_norm(n, transposed):
                if n % 3 == 1:
                    pool.wait_ge(*product((n // 3, "xw", 3)))
                load_gains(n)
                pool.wait_ge(ln_loaded, 32 * (n + 1))
                pool.wait_ge(*product(transposed + (3,)))
                if n != 3 * DEPTH - 2:
                    link(gain_and_bias(0))
                gain_and_bias(1).then_inc(ln_pool, 1)
                pool.wait_ge(ln_pool, n + 1)

            for l in range(DEPTH):
                if l:
                    zero_offdiagonal(l)
                load(gain[:, :], t["gla_gain"][l:l + 1, :].to_broadcast((P, BRANCH)), gain_loaded)
                if l:
                    layer_norm(2, ("xT", 1, 0))
                pool.wait_ge(*product((l, "ybT", 1)))
                pool.dma_start(mem_tok[:, :, :], t["mem"].rearrange("o (t p) d -> p (o t) d", p=P))\
                    .then_inc(mem_loaded, 16)
                pool.wait_ge(*product((l, "branch", 1, 2)))
                layer_norm(3 * l, ("xT", l, 1))
                layer_norm(3 * l + 1, ("xT", l, 2))
            for i in range(TT):
                pool.wait_ge(xtok_hi_ready, i + 1)
                link(pool.tensor_tensor(xtok_lo[:, i, :], x[:, i, :], xtok_hi[:, i, :].bitcast(F32), ALU.subtract))
            pool.sem_inc(xtok_ready, 1)
            pool.wait_ge(ln_dve, 1)
            pool.wait_ge(step_done, route.step_no["logits"] + 1)
            pool.tensor_scalar(acc[:, :, :], x[:, :, :], ALPHA, None, ALU.mult).then_inc(acc_ready, 1)
            pool.wait_ge(acc_ready, 1)
            pool.wait_ge(rounds_done, 1)
            load_gains(3 * DEPTH - 1, last_gb)
            pool.wait_ge(ln_loaded, 32 * 3 * DEPTH)
            pool.wait_ge(act_normed, 6 * DEPTH)
            part = x[:, 1, 0:POOL_PART]
            link(pool.tensor_tensor(part, part, last_gb[:, 0, 0:POOL_PART], ALU.mult))
            pool.tensor_tensor(part, part, last_gb[:, 1, 0:POOL_PART], ALU.add).then_inc(ln_pool, 1)
            pool.wait_ge(ln_pool, 3 * DEPTH)

        @block.scalar
        def _(act):
            act.dma_start(mats[:, :, :], t["c_mats"].rearrange("i p n -> p i n")).then_inc(mats_loaded, 16)
            split = [0]
            links = [0]

            def link(ins):
                links[0] += 1
                ins.then_inc(act_link, 1)
                act.wait_ge(act_link, links[0])

            def round_until(n):
                for u in range(split[0], min(n, U0)):
                    act.wait_ge(raw_loaded[u % RAW], raw_target[u])
                    if u >= SPLIT:
                        act.wait_ge(unit_done, u - SPLIT + 1)
                    f = dense.units[u][1]
                    act.activation(w_hi[:, u % SPLIT, 0:f], raw[:, u % RAW, 0:f], ACT.Copy).then_inc(hi_ready, 1)
                split[0] = max(split[0], n)

            def ready(key):
                round_until(dense.before[key] + SPLIT)
                act.wait_ge(*product(key))

            def done(ins, key, i=0):
                ins.then_inc(drained[dense.bank[key][i][0]], 1)

            def pb(key, i=0):
                return bank[dense.bank[key][i][0]]

            def normalize(n, src=x):
                act.wait_ge(var_ready, n + 1)
                act.activation(rstd[:, :], nmr[:, :], ACT.Sqrt).then_inc(sqrt_ready, 1)
                act.wait_ge(scale_ready, n + 1)
                for h in range(2):
                    cols = slice(512 * h, 512 * h + 512)
                    act.activation(x[:, 1, cols], src[:, 1, cols], ACT.Identity, scale=rstd[:, 1:2], bias=nmr[:, 1:2])\
                       .then_inc(act_normed, 1)

            def round_product(key, dst, ahead=SPLIT):
                round_until(dense.before[key] + ahead)
                act.wait_ge(*product(key))
                i = key[-1]
                act.activation(dst[:, 2 * i:2 * i + 2, :], pb(key)[:, :].rearrange("p (k t) -> p k t", k=2), ACT.Copy)\
                   .then_inc(rounded, 1)

            def normalized_features(l, w, n, ahead=SPLIT):
                for i in range(4):
                    key = ("xT", l, w, i)
                    round_until(dense.before[key] + ahead)
                    act.wait_ge(*product(key))
                    for k in range(2):
                        kk = 2 * i + k
                        ins = act.activation(xn[:, i, k, :], pb(key)[:, T * k:T * k + T], ACT.Identity,
                                             scale=ln_f[:, 0, n, kk:kk + 1], bias=ln_f[:, 1, n, kk:kk + 1])
                    ins.then_inc(rounded, 1)

            for i in range(4):
                round_product(("xT", 0, 0, i), xT_hi, ahead=1)
            for l in range(DEPTH):
                ready((l, "vT"))
                done(act.activation(vwin[:, :, :], pb((l, "vT"))[:, 0:3 * P], ACT.Copy), (l, "vT"))
                act.wait_ge(zeroed, l + 2)
                for n in range(2):
                    ready((l, "q", n))
                    src = pb((l, "q", n))[:, :].rearrange("p (t c i) -> p t c i", t=2, c=NC)
                    act.activation(q_bd[0:64, 2 * n:2 * n + 2, :, 0:64], src[0:64], ACT.Copy, scale=CHUNK ** -0.5)
                    done(act.activation(q_bd[64:P, 2 * n:2 * n + 2, :, 64:P], src[64:P], ACT.Copy,
                                        scale=CHUNK ** -0.5), (l, "q", n))
                ready((l, "bv", 0))
                if l:
                    act.wait_ge(ln_pool, 3)
                done(act.activation(bv[:, :, 0:256], pb((l, "bv", 0))[:, :], ACT.Copy), (l, "bv", 0))
                ready((l, "bv", 1))
                done(act.activation(bv[:, :, 256:512], pb((l, "bv", 1))[:, :], ACT.Copy), (l, "bv", 1))
                ready((l, "z"))
                link(act.activation(kdec[:, 0, :, :], pb((l, "z"))[:, :], ACT.Abs))
                link(act.activation(kdec[:, 0, :, :], kdec[:, 0, :, :], ACT.Exp, scale=-1.0))
                act.activation(log_a[:, :, :], kdec[:, 0, :, :], ACT.Ln, bias=1.0).then_inc(log1p_ready, 1)
                ready((l, "bq"))
                done(act.activation(bqT[:, :, :], pb((l, "bq"))[:, :], ACT.Copy, scale=CHUNK ** -0.5), (l, "bq"))
                act.wait_ge(shifted, l + 1)
                act.activation(prob[:, :, :, :], prob[:, :, :, :], ACT.Exp)
                act.activation(sk[:, :, :], sk[:, :, :], ACT.Exp).then_inc(expd, 1)
                def branch_gate(n):
                    ready((l, "br", n))
                    done(act.activation(br[:, :, 256 * n:256 * n + 256], pb((l, "br", n))[:, :], ACT.Silu),
                         (l, "br", n))

                branch_gate(0)
                ready((l, "cum"))
                done(act.activation(kdec[:, 0, :, :], pb((l, "cum"))[:, :], ACT.Exp), (l, "cum"))
                ready((l, "end"))
                act.activation(dec[:, :, :], pb((l, "end"))[:, 0:2 * NC], ACT.Exp).then_inc(decay_ready, 1)
                branch_gate(1)
                for c in range(NC):
                    ready((l, "pT", c))
                    done(act.activation(probT[:, c, :], pb((l, "pT", c))[:, :], ACT.Copy), (l, "pT", c))
                for n in range(2):
                    ready((l, "cc", n))
                    done(act.activation(cc[:, 2 * n:2 * n + 2, :], pb((l, "cc", n))[:, :], ACT.Copy), (l, "cc", n))
                for i in range(TT):
                    ready((l, "gla", i))
                    act.wait_ge(state_ready, l * NC + NC)
                    done(act.activation(gla[:, i, :], pb((l, "gla", i))[:, :], ACT.Copy), (l, "gla", i))
                act.wait_ge(gla_ms, l + 1)
                act.activation(ms[:, :, :], ms[:, :, :], ACT.Sqrt).then_inc(gla_sqrt, 1)
                act.wait_ge(const_loaded, CONSTS)
                for half in range(2):
                    for b in range(3):
                        n = (l * 2 + half) * 3 + b
                        if n % 6 >= 2 or l:
                            act.wait_ge(gate_used, n - 1)
                        for i in range(2):
                            key = (l, "gate", half, b, i)
                            ready(key)
                            for j in range(2):
                                tile = b * KD + 4 * half + 2 * i + j
                                ins = act.activation(gates[:, n % 2, 2 * i + j, :], pb(key)[:, T * j:T * j + T],
                                                     ACT.Sigmoid, bias=b_gate[:, l, tile:tile + 1])
                            done(ins, key)
                for n in range(4):
                    round_product((l, "memT", n), memT_hi)
                round_until(dense.before[(l, "out", 3)] + SPLIT)
                normalize(3 * l)
                for n in range(l, 4):
                    ready((l, "xk", n))
                    done(act.activation(xkT[:, 2 * n:2 * n + 2, :], pb((l, "xk", n))[:, :], ACT.Copy), (l, "xk", n))
                normalized_features(l, 1, 3 * l)

                def xattn_v(n):
                    ready((l, "xv", n))
                    done(act.activation(xv[:, :, 256 * n:256 * n + 256], pb((l, "xv", n))[:, :], ACT.Copy), (l, "xv", n))

                def xattn_scores(h):
                    ready((l, "xs", h))
                    act.wait_ge(xmax_ready, 4 * l + h + 1)
                    src = pb((l, "xs", h))
                    act.activation(xprob[:, h, 0, :], src[:, 0:T], ACT.Exp, bias=xmx[:, h, 0:1],
                                   accum_out=xsum[:, h, 0:1])
                    act.activation(xprob[:, h, 1, :], src[:, T:2 * T], ACT.Exp, bias=xmx[:, h, 1:2],
                                   accum_out=xsum[:, h, 1:2]).then_inc(xexp_ready, 1)

                def xattn_probT(h):
                    ready((l, "xp", h))
                    done(act.activation(xprobT[:, h, :, :], pb((l, "xp", h))[:, :], ACT.Copy), (l, "xp", h))

                def xattn_q(n):
                    ready((l, "xq", n))
                    done(act.activation(xqT[:, 2 * n:2 * n + 2, :], pb((l, "xq", n))[:, :], ACT.Copy, scale=T ** -0.5),
                         (l, "xq", n))

                xattn_v(0)
                xattn_v(1)
                xattn_q(0)
                xattn_q(1)
                xattn_scores(0)
                xattn_q(2)
                xattn_scores(1)
                xattn_probT(0)
                xattn_q(3)
                xattn_scores(2)
                xattn_probT(1)
                xattn_v(2)
                xattn_scores(3)
                xattn_probT(2)
                xattn_v(3)
                xattn_probT(3)
                round_until(dense.before[(l, "xw", 3)] + 2)
                normalize(3 * l + 1)
                normalized_features(l, 2, 3 * l + 1, ahead=2 if l else 1)
                if l == 0:
                    key = (1, "xk", 0)
                    act.wait_ge(*product(key))
                    done(act.activation(xk_early[:, :, :], pb(key)[:, :], ACT.Copy), key)
                if l == 0:
                    for n in range(FF // 256):
                        ready((l, "fg", n))
                        if n >= 2:
                            act.wait_ge(h_ready, n - 1)
                        done(act.activation(fsilu[:, n % 2, :], pb((l, "fg", n))[:, :], ACT.Silu)
                             , (l, "fg", n))
                    round_until(dense.before[(l, "ffn")] + 2)
                    normalize(2)
                    normalized_features(1, 0, 2, ahead=2)
            round_until(U0)

            def round_units(prev, i0, i1):
                for i in range(i0, i1):
                    u = U0 + i
                    per = 16 * E_UNITS // E_RAW
                    slot, place = expert_raw(i)
                    act.wait_ge(raw_loaded[slot], rounds(prev, per, per, raw_base[slot] + 16 * (i // E_RAW + 1)))
                    act.wait_ge(unit_done, rounds(prev, E_UNITS, E_UNITS, u - SPLIT + 1))
                    act.activation(w_hi[:, u % SPLIT, :], place, ACT.Copy).then_inc(hi_ready, 1)

            round_units(None, 0, SPLIT)
            for i in range(TT):
                act.wait_ge(*((ln_dve, 1) if i == 0 else (ln_pool, 3 * DEPTH - 1)))
                act.activation(xtok_hi[:, i, :], x[:, i, :], ACT.Copy).then_inc(xtok_hi_ready, 1)
            act.wait_ge(top_ready, 1)
            act.activation(wts[:, :, 1], wts[:, :, 1], ACT.Exp).then_inc(exp_top, 1)
            HF = FF // 256

            def expert(prev):
                plan = first if prev is None else rnd
                done_to = [SPLIT if prev is None else 0]

                def round_to(n):
                    round_units(prev, done_to[0], min(n, E_UNITS))
                    done_to[0] = max(done_to[0], n)

                def wait_step(key):
                    act.wait_ge(step_done, rounds(prev, first.steps, rnd.steps, S0 + plan.step_no[key] + 1))

                if prev is not None:
                    round_to(2)
                    act.wait_ge(unit_done, rounds(prev, E_UNITS, E_UNITS, U0))
                    for i in range(2):
                        act.activation(ye_hi[:, 512 * i:512 * i + 512], bank[6 + i][:, :], ACT.Copy).then_inc(y_hi_ready, 1)
                for j in range(GU_STEPS):
                    n = plan.unit_no[("g", j, 1)]
                    round_to(n + 1 + 2)
                    act.wait_ge(unit_done, rounds(prev, E_UNITS, E_UNITS, U0 + n + 1))
                    b = 2 * (j % 2)
                    act.wait_ge(h_ready, rounds(prev, GU_STEPS, GU_STEPS, HF + j - 1))
                    act.activation(esilu[:, j % 2, :], bank[b][:, :], ACT.Silu).then_inc(drained[b], 1)
                    if j == 0:
                        continue
                    round_to(plan.before[("hT", j - 1)] + 2)
                    wait_step(("hT", j - 1))
                    act.activation(eT_hi[:, 4 * j - 4:4 * j, :], bank[4 + j % 2][:, :], ACT.Copy).then_inc(hT_hi_ready, 1)
                    if j == 1:
                        wait_step("selT")
                        act.activation(selT[:, :, :], bank[6][:, 0:T], ACT.Copy).then_inc(drained[6], 1)
                round_to(plan.before[("hT", GU_STEPS - 1)] + 2)
                wait_step(("hT", GU_STEPS - 1))
                act.activation(eT_hi[:, EK - 4:EK, :], bank[5][:, :], ACT.Copy).then_inc(hT_hi_ready, 1)
                round_to(plan.before["dispatch"] + 2)
                wait_step("dispatch")
                for i in range(2):
                    act.activation(xe_hi[:, 4 * i:4 * i + 4, :], bank[i][:, :], ACT.Copy).then_inc(drained[i], 1)
                round_to(E_UNITS)

            act.wait_ge(step_done, route.step_no["dispatch"] + 1)
            for i in range(2):
                act.activation(xe_hi[:, 4 * i:4 * i + 4, :], bank[i][:, :], ACT.Copy).then_inc(drained[i], 1)
            expert(None)
            with act.Fori(0, EXPERTS - 1) as e:
                expert(e)
            act.wait_ge(routed, 1)
            over = act.value_load(ovi[0:1, 0:1], min_val=0, max_val=OVER)
            with act.If(over > 0):
                with act.Fori(0, OVER) as m:
                    expert(m + (EXPERTS - 1))
            act.wait_ge(rounds_done, 1)
            for i in range(2):
                act.activation(ye_hi[:, 512 * i:512 * i + 512], bank[6 + i][:, :], ACT.Copy).then_inc(last_y_hi, 1)
            normalize(5, acc)

        @block.vector
        def _(dve):
            split = [0]
            links = [0]

            def link(ins):
                links[0] += 1
                ins.then_inc(dve_link, 1)
                dve.wait_ge(dve_link, links[0])

            def rest_until(n):
                for u in range(split[0], min(n, U0)):
                    dve.wait_ge(hi_ready, u + 1)
                    f = dense.units[u][1]
                    dve.tensor_tensor(w_lo[:, u % SPLIT, 0:f], raw[:, u % RAW, 0:f],
                                      w_hi[:, u % SPLIT, 0:f].bitcast(F32), ALU.subtract).then_inc(lo_ready, 1)
                split[0] = max(split[0], n)

            def ready(key, ahead=SPLIT):
                rest_until(dense.before[key] + ahead)
                dve.wait_ge(*product(key))

            def done(ins, key, i=0):
                ins.then_inc(drained[dense.bank[key][i][0]], 1)

            def pb(key, i=0):
                return bank[dense.bank[key][i][0]]

            def split_to(hi, lo, src):
                link(dve.tensor_copy(hi, src))
                return dve.tensor_tensor(lo, src, hi.bitcast(F32), ALU.subtract)

            def rest_of(key, hi, lo, ahead=SPLIT):
                ready(key, ahead)
                dve.wait_ge(rounded, dense.rounded[key])
                i = key[-1]
                done(dve.tensor_tensor(lo[:, 2 * i:2 * i + 2, :], pb(key)[:, :].rearrange("p (k t) -> p k t", k=2),
                                       hi[:, 2 * i:2 * i + 2, :].bitcast(F32), ALU.subtract), key)

            def split_features(l, w, ahead=SPLIT):
                for i in range(4):
                    key = ("xT", l, w, i)
                    ready(key, ahead)
                    dve.wait_ge(rounded, dense.rounded[key])
                    done(split_to(xT_hi[:, 2 * i:2 * i + 2, :], xT_lo[:, 2 * i:2 * i + 2, :], xn[:, i, :, :]), key)

            def layer_norm(n, parts, src=x):
                for i in range(TT):
                    ins = dve.bn_aggr(mv[:, i, :], stats[:, i, 0:parts, :].rearrange("p a b -> p (a b)"))
                link(ins)
                dve.tensor_scalar(nmr[:, :], mv[:, :, 1], LN_EPS, None, ALU.add).then_inc(var_ready, 1)
                dve.wait_ge(sqrt_ready, n + 1)
                link(dve.reciprocal(rstd[:, :], rstd[:, :]))
                dve.scalar_tensor_tensor(out=nmr[:, :], in0=mv[:, :, 0], scalar=-1.0, in1=rstd[:, :],
                                         op0=ALU.mult, op1=ALU.mult).then_inc(scale_ready, 1)
                for h in range(2):
                    cols = slice(512 * h, 512 * h + 512)
                    dve.tensor_scalar(x[:, 0, cols], src[:, 0, cols], mv[:, 0, 0:1], rstd[:, 0:1], ALU.subtract, ALU.mult)\
                       .then_inc(dve_normed, 1)

            def add_residual(key, n, ahead=SPLIT):
                ready(key, ahead)
                dst = x[:, :, 256 * n:256 * n + 256]
                done(dve.scalar_tensor_tensor(out=dst, in0=dst, scalar=ALPHA,
                                              in1=pb(key)[:, :].rearrange("p (t n) -> p t n", t=TT),
                                              op0=ALU.mult, op1=ALU.add), key)
                b, m = dense.bank[key][0]
                dve.wait_ge(drained[b], m + 1)
                for i in range(TT):
                    ins = dve.bn_stats(stats[:, i, n, :], x[:, i, 256 * n:256 * n + 256])
                link(ins)

            for i in range(4):
                rest_of(("xT", 0, 0, i), xT_hi, xT_lo, ahead=1)
            ready("bias", ahead=1)
            done(dve.tensor_copy(diag[:, :], pb("bias")[0:SWA_HEADS, 0:REL]), "bias")
            b, m = dense.bank["bias"][0]
            dve.wait_ge(drained[b], m + 1)
            dve.sem_inc(bias_diag, 1)

            for l in range(DEPTH):
                key = (l, "kv")
                ready(key)
                dve.tensor_copy(kT[:, :], pb(key)[:, 0:T])
                done(dve.tensor_copy(vT[:, :], pb(key)[:, T:2 * T]), key)
                key = (l, "bk")
                ready(key)
                done(dve.tensor_copy(bk[:, :, :], pb(key)[:, :].rearrange("p (t n) -> p t n", t=TT)), key)
                link(dve.memset(lrT[0:32, :], 1.0))
                key = (l, "lr")
                ready(key)
                done(dve.tensor_copy(lrT[0:RANK, :], pb(key)[0:RANK, 0:T]), key)
                for c in range(NC):
                    key = (l, "scores", c)
                    ready(key)
                    if c == 0:
                        dve.wait_ge(bias_loaded, 32)
                    src = pb(key)[:, :].rearrange("p (t j) -> p t j", t=PAIRS)
                    if c:
                        done(dve.tensor_tensor(prob[:, c, :, :], src, bias[:, :, :], ALU.add), key)
                    else:
                        dve.tensor_tensor(prob[:, 0, :, 0:64], src[:, :, 0:64], bias[:, :, 64:P], ALU.add)
                        done(dve.tensor_scalar(prob[:, 0, :, 64:P], src[:, :, 64:P], 0.0, NEG, ALU.mult, ALU.add), key)
                b, n = dense.bank[(l, "scores", NC - 1)][0]
                dve.wait_ge(drained[b], n + 1)
                dve.wait_ge(const_loaded, CONSTS)
                link(dve.tensor_reduce(mx[:, :, :], prob[:, :, :, :], AX.X, ALU.max))
                sink_b = sink[:, l:l + 1, :].to_broadcast((P, NC, PAIRS))
                link(dve.tensor_tensor(mx[:, :, :], mx[:, :, :], sink_b, ALU.max))
                dve.tensor_tensor(sk[:, :, :], sink_b, mx[:, :, :], ALU.subtract)
                dve.tensor_tensor(prob[:, :, :, :].rearrange("p c t j -> p (c t) j"),
                                  prob[:, :, :, :].rearrange("p c t j -> p (c t) j"),
                                  mx[:, :, :].rearrange("p c t -> p (c t)").unsqueeze(2).to_broadcast((P, NC * PAIRS, P)),
                                  ALU.subtract).then_inc(shifted, 1)
                key = (l, "z")
                ready(key)
                dve.wait_ge(log1p_ready, l + 1)
                done(dve.scalar_tensor_tensor(out=log_a[:, :, :], in0=pb(key)[:, :].rearrange("p (t n) -> p t n", t=TT),
                                              scalar=0.0, in1=log_a[:, :, :], op0=ALU.min, op1=ALU.subtract), key)
                if l == 0:
                    link(dve.tensor_copy(w_rt2[:, :, 0, :], w_rt[:, :, :]))
                    dve.tensor_tensor(w_rt2[:, :, 1, :], w_rt[:, :, :], w_rt2[:, :, 0, :].bitcast(F32), ALU.subtract)\
                       .then_inc(router_ready, 1)
                rest_until(dense.before[(l, "bq")] + SPLIT)
                dve.wait_ge(expd, l + 1)
                link(dve.tensor_reduce(rs[:, :, :], prob[:, :, :, :], AX.X, ALU.add))
                link(dve.tensor_tensor(rs[:, :, :], rs[:, :, :], sk[:, :, :], ALU.add))
                link(dve.reciprocal(rs[:, :, :], rs[:, :, :]))
                dve.tensor_tensor(prob[:, :, :, :].rearrange("p c t j -> p (c t) j"),
                                  prob[:, :, :, :].rearrange("p c t j -> p (c t) j"),
                                  rs[:, :, :].rearrange("p c t -> p (c t)").unsqueeze(2).to_broadcast((P, NC * PAIRS, P)),
                                  ALU.mult).then_inc(normed, 1)
                key = (l, "end")
                ready(key)
                dve.wait_ge(decay_ready, l + 1)
                dve.sem_inc(drained[dense.bank[key][0][0]], 1)
                dve.scalar_tensor_tensor(out=kdec[:, 1, :, :], in0=bk[:, :, :], scalar=ind[:, 3:4],
                                         in1=kdec[:, 0, :, :], op0=ALU.mult, op1=ALU.mult).then_inc(kdec_ready, 1)
                dve.wait_ge(kdec_ready, 2 * l + 1)
                dve.scalar_tensor_tensor(out=kdec[:, 0, :, :], in0=bk[:, :, :], scalar=ind[:, 2:3],
                                         in1=kdec[:, 0, :, :], op0=ALU.mult, op1=ALU.mult).then_inc(kdec_ready, 1)
                dve.wait_ge(zeroed, l + 2)
                for c in range(NC):
                    key = (l, "state", c)
                    ready(key)
                    if c == 0:
                        dve.wait_ge(decay_ready, l + 1)
                    else:
                        dve.wait_ge(state_ready, l * NC + c)
                    for p2 in range(2):
                        for g in range(2):
                            rows, cols = slice(64 * g, 64 * g + 64), slice(P * g, P * g + P)
                            src = pb(key)[rows, T * p2 + P * g:T * p2 + P * g + P]
                            if c == 0:
                                ins = dve.tensor_copy(state[rows, 0, p2, cols], src)
                            else:
                                ins = dve.scalar_tensor_tensor(out=state[rows, c, p2, cols],
                                                               in0=state[rows, c - 1, p2, cols],
                                                               scalar=dec[rows, p2, c:c + 1], in1=src,
                                                               op0=ALU.mult, op1=ALU.add)
                    ins.then_inc(state_ready, 1)
                    dve.wait_ge(state_ready, l * NC + c + 1)
                    dve.sem_inc(drained[dense.bank[key][0][0]], 1)
                for c in range(NC):
                    key = (l, "pv", c)
                    ready(key)
                    src = pb(key)[:, :].rearrange("p (t n) -> p t n", t=PAIRS)
                    toks = slice(CHUNK * c, CHUNK * c + CHUNK)
                    dve.tensor_copy(y_hi[0:64, 0, :, toks], src[0:64, :, 0:64])
                    link(dve.tensor_copy(y_hi[64:P, 0, :, toks], src[64:P, :, 64:P]))
                    dve.tensor_tensor(y_lo[0:64, 0, :, toks], src[0:64, :, 0:64],
                                      y_hi[0:64, 0, :, toks].bitcast(F32), ALU.subtract)
                    done(dve.tensor_tensor(y_lo[64:P, 0, :, toks], src[64:P, :, 64:P],
                                           y_hi[64:P, 0, :, toks].bitcast(F32), ALU.subtract), key)

                def conv_input(n):
                    b, m = dense.bank[(l, "cc", n)][0]
                    key = (l, "ch", n)
                    ready(key)
                    dve.wait_ge(drained[b], m + 1)
                    done(dve.tensor_tensor(cu[:, 2 * n:2 * n + 2, 2:2 + T], pb(key)[:, :].rearrange("p (c t) -> p c t", c=2),
                                           cc[:, 2 * n:2 * n + 2, :], ALU.mult), key)

                dve.wait_ge(*product((l, "pT", NC - 1)))
                link(dve.memset(cu[:, :, 0:2], 0.0))
                conv_input(0)
                rest_until(dense.before[(l, "gla", 1)] + SPLIT)
                for i in range(TT):
                    b, n = dense.bank[(l, "gla", i)][0]
                    dve.wait_ge(drained[b], n + 1)
                link(dve.tensor_tensor(sq[:, :, :], gla[:, :, :], gla[:, :, :], ALU.mult))
                link(dve.tensor_reduce(ms[:, :, :], sq[:, :, :].rearrange("p t (h v) -> p t h v", h=4), AX.X, ALU.add))
                dve.tensor_scalar(ms[:, :, :], ms[:, :, :], 1.0 / P, LN_EPS, ALU.mult, ALU.add).then_inc(gla_ms, 1)
                dve.wait_ge(gain_loaded, 16 * (l + 1))
                b, n = dense.bank[(l, "br", 1)][0]
                dve.wait_ge(drained[b], n + 1)
                dve.tensor_tensor(br[:, :, :], br[:, :, :], gain[:, :].unsqueeze(1).to_broadcast((P, TT, BRANCH)), ALU.mult)\
                   .then_inc(dve_link, 1)
                links[0] += 1
                dve.wait_ge(gla_sqrt, l + 1)
                link(dve.reciprocal(ms[:, :, :], ms[:, :, :]))
                link(dve.tensor_tensor(gla[:, :, :].rearrange("p t (h v) -> p (t h) v", h=4),
                                       gla[:, :, :].rearrange("p t (h v) -> p (t h) v", h=4),
                                       ms[:, :, :].rearrange("p t h -> p (t h)").unsqueeze(2).to_broadcast((P, TT * 4, P)),
                                       ALU.mult))
                dve.tensor_tensor(gla[:, :, :], gla[:, :, :], br[:, :, :], ALU.mult).then_inc(yb_ready, 1)
                conv_input(1)
                b, n = dense.bank[(l, "ch", 1)][0]
                dve.wait_ge(drained[b], n + 1)
                for k in range(3):
                    for c in range(KB):
                        w = w_conv[:, l, k, c:c + 1]
                        src = cu[:, c, k:k + T]
                        if k == 0:
                            ins = dve.tensor_scalar(cy[:, c, :], src, w, None, ALU.mult)
                        else:
                            ins = dve.scalar_tensor_tensor(out=cy[:, c, :], in0=src, scalar=w, in1=cy[:, c, :],
                                                           op0=ALU.mult, op1=ALU.add)
                    link(ins)
                for n in range(2):
                    key = (l, "cb", n)
                    ready(key)
                    done(dve.tensor_tensor(cy[:, 2 * n:2 * n + 2, :], pb(key)[:, :].rearrange("p (c t) -> p c t", c=2),
                                           cy[:, 2 * n:2 * n + 2, :], ALU.mult), key)
                for i in range(2):
                    key = (l, "ybT", i)
                    ready(key)
                    done(split_to(y_hi[:, 1, 2 * i:2 * i + 2, :], y_lo[:, 1, 2 * i:2 * i + 2, :],
                                  pb(key)[:, :].rearrange("p (k t) -> p k t", k=2)), key)
                for n in range(2):
                    b, m = dense.bank[(l, "cb", n)][0]
                    dve.wait_ge(drained[b], m + 1)
                split_to(y_hi[:, 2, :, :], y_lo[:, 2, :, :], cy[:, :, :]).then_inc(y_ready, 1)
                dve.wait_ge(y_ready, l + 1)
                for half in range(2):
                    for br_no in range(3):
                        n = (l * 2 + half) * 3 + br_no
                        key = (l, "branch", half, br_no)
                        for i in range(2):
                            b, m = dense.bank[(l, "gate", half, br_no, i)][0]
                            rest_until(dense.before[(l, "gate", half, br_no, i)] + SPLIT)
                            dve.wait_ge(drained[b], m + 1)
                        ready(key, ahead=2 if (half, br_no) == (1, 2) else SPLIT)
                        if br_no == 0:
                            for i in range(2):
                                done(dve.tensor_tensor(msum[:, 2 * i:2 * i + 2, :],
                                                       pb(key, i)[:, :].rearrange("p (c t) -> p c t", c=2),
                                                       gates[:, n % 2, 2 * i:2 * i + 2, :], ALU.mult), key, i)
                            for i in range(2):
                                b, m = dense.bank[key][i]
                                dve.wait_ge(drained[b], m + 1)
                            dve.sem_inc(gate_used, 1)
                            continue
                        for i in range(2):
                            g = gates[:, n % 2, 2 * i:2 * i + 2, :]
                            m_i = msum[:, 2 * i:2 * i + 2, :]
                            done(dve.tensor_tensor(g, pb(key, i)[:, :].rearrange("p (c t) -> p c t", c=2), g, ALU.mult),
                                 key, i)
                            b, m = dense.bank[key][i]
                            dve.wait_ge(drained[b], m + 1)
                            link(dve.tensor_tensor(m_i, m_i, g, ALU.add))
                            if br_no == 2:
                                k = 4 * half + 2 * i
                                split_to(merged_hi[:, k:k + 2, :], merged_lo[:, k:k + 2, :], m_i).then_inc(merged_ready, 1)
                                dve.wait_ge(merged_ready, 4 * l + 2 * half + i + 1)
                        dve.sem_inc(gate_used, 1)
                for n in range(4):
                    rest_of((l, "memT", n), memT_hi, memT_lo)
                if l:
                    dve.wait_ge(ln_pool, 3)
                for n in range(4):
                    add_residual((l, "out", n), n)
                layer_norm(3 * l, 4)
                split_features(l, 1)
                rest_until(dense.before[(l, "xv", 1)] + SPLIT)

                def xattn_max(h):
                    key = (l, "xs", h)
                    ready(key)
                    dve.tensor_reduce(xmx[:, h, :], pb(key)[:, :].rearrange("p (t m) -> p t m", t=TT), AX.X, ALU.max,
                                      negate=True).then_inc(xmax_ready, 1)

                def xattn_prob(h):
                    dve.wait_ge(xexp_ready, 4 * l + h + 1)
                    link(dve.reciprocal(xrec[:, h, :], xsum[:, h, :]))
                    dve.sem_inc(drained[dense.bank[(l, "xs", h)][0][0]], 1)
                    for i in range(TT):
                        ins = dve.tensor_scalar(xprob[:, h, i, :], xprob[:, h, i, :], xrec[:, h, i:i + 1], None, ALU.mult)
                    ins.then_inc(xprob_ready, 1)

                def xattn_out(h):
                    key = (l, "xo", h)
                    ready(key)
                    done(split_to(xoT_hi[:, 2 * h:2 * h + 2, :], xoT_lo[:, 2 * h:2 * h + 2, :],
                                  pb(key)[:, :].rearrange("p (k t) -> p k t", k=2)), key)

                xattn_max(0)
                xattn_prob(0)
                xattn_max(1)
                xattn_prob(1)
                xattn_max(2)
                xattn_prob(2)
                dve.wait_ge(ln_pool, 3 * l + 1)
                xattn_out(0)
                xattn_max(3)
                xattn_prob(3)
                for h in range(1, 4):
                    xattn_out(h)
                dve.wait_ge(ln_pool, 3 * l + 1)
                for n in range(4):
                    add_residual((l, "xw", n), n, ahead=1 if n == 3 else SPLIT)
                layer_norm(3 * l + 1, 4)
                split_features(l, 2, ahead=2 if l else 1)
                if l:
                    continue
                for n in range(FF // 256):
                    b, m = dense.bank[(l, "fg", n)][0]
                    key = (l, "fu", n)
                    ready(key)
                    dve.wait_ge(drained[b], m + 1)
                    done(dve.tensor_tensor(fprod[:, n % 2, :], pb(key)[:, :], fsilu[:, n % 2, :], ALU.mult), key)
                    b, m = dense.bank[key][0]
                    dve.wait_ge(drained[b], m + 1)
                    src = fprod[:, n % 2, :].rearrange("p (k t) -> p k t", k=2)
                    split_to(hT_hi[:, 2 * n:2 * n + 2, :], hT_lo[:, 2 * n:2 * n + 2, :], src).then_inc(h_ready, 1)
                    dve.wait_ge(h_ready, n + 1)
                key = (l, "ffn")
                rest_until(dense.before[key] + 1)
                dve.wait_ge(ln_pool, 2)

                def ffn_stats(i, h):
                    b, m = dense.bank[key][2 * i + h]
                    dve.wait_ge(drained[b], m + 1)
                    return dve.bn_stats(stats[:, i, h, :], x[:, i, 512 * h:512 * h + 512])

                for i in range(TT):
                    for h in range(2):
                        if (i, h) == (1, 1):
                            link(ffn_stats(1, 0))
                            dve.wait_ge(*product(key))
                        else:
                            dve.wait_ge(ffn_done, 2 * i + h + 1)
                        dst = x[:, i, 512 * h:512 * h + 512]
                        done(dve.scalar_tensor_tensor(out=dst, in0=dst, scalar=ALPHA, in1=pb(key, 2 * i + h)[:, :],
                                                      op0=ALU.mult, op1=ALU.add), key, 2 * i + h)
                        if (i, h) in ((0, 1), (1, 0)):
                            ffn_stats(*divmod(2 * i + h - 1, 2))
                link(ffn_stats(1, 1))
                layer_norm(2, 2)
                split_features(1, 0, ahead=2)

            rest_until(U0)
            def rest_units(prev, i0, i1):
                for i in range(i0, i1):
                    u = U0 + i
                    dve.wait_ge(hi_ready, rounds(prev, E_UNITS, E_UNITS, u + 1))
                    dve.tensor_tensor(w_lo[:, u % SPLIT, :], expert_raw(i)[1], w_hi[:, u % SPLIT, :].bitcast(F32),
                                      ALU.subtract).then_inc(lo_ready, 1)

            dve.wait_ge(ln_loaded, 32 * (3 * DEPTH - 1))
            link(dve.tensor_tensor(x[:, 0, :], x[:, 0, :], ln_gb[:, 0, :], ALU.mult))
            dve.tensor_tensor(x[:, 0, :], x[:, 0, :], ln_gb[:, 1, :], ALU.add).then_inc(ln_dve, 1)
            rest_units(None, 0, 2)
            dve.wait_ge(step_done, route.step_no["logits"] + 1)
            for i in range(TT):
                ins = dve.tensor_tensor(lg[:, i, :], bank[4 + 2 * i][:, 0:EXPERTS], b_rt[:, :], ALU.add)
            link(ins)
            for i in range(TT):
                dve.tensor_tensor(lg[:, i, :], bank[4 + 2 * i][:, EXPERTS:2 * EXPERTS], lg[:, i, :], ALU.add)\
                   .then_inc(drained[4 + 2 * i], 1)
            for b, n in route.bank["logits"]:
                dve.wait_ge(drained[b], n + 1)
            for i in range(TT):
                ins = dve.max(top[:, i, :], lg[:, i, :])
            link(ins)
            for i in range(TT):
                ins = dve.max_index(topi[:, i, :], top[:, i, :], lg[:, i, :])
            link(ins)
            link(dve.tensor_copy(topf[:, :, :], topi[:, :, :]))
            experts = iota8.unsqueeze(1).to_broadcast((P, TT, EXPERTS))
            dve.tensor_tensor(pick[:, :, :], experts, topf[:, :, 0:1].to_broadcast((P, TT, EXPERTS)), ALU.is_equal)
            link(dve.tensor_tensor(pick2[:, :, :], experts, topf[:, :, 1:2].to_broadcast((P, TT, EXPERTS)), ALU.is_equal))
            dve.tensor_tensor(picked[:, :, :], pick[:, :, :], pick2[:, :, :], ALU.add).then_inc(picked_ready, 1)
            dve.tensor_tensor(wts[:, :, 1], top[:, :, 1], top[:, :, 0], ALU.subtract).then_inc(top_ready, 1)
            link(dve.memset(wtab[:, :, :], 0.0))
            link(dve.memset(pos[:, :, :], -1.0))
            dve.wait_ge(step_done, route.step_no["ranks"] + 1)
            dve.wait_ge(picked_ready, 1)
            dve.scalar_tensor_tensor(out=tmp8[:, :, :], in0=bank[5][:, 0:TT * EXPERTS].rearrange("p (t e) -> p t e", t=TT),
                                     scalar=1.0, in1=picked[:, :, :], op0=ALU.add, op1=ALU.mult).then_inc(drained[5], 1)
            dve.wait_ge(drained[5], route.bank["ranks"][0][1] + 1)
            link(dve.tensor_scalar(pos[:, :, 0:EXPERTS], tmp8[:, :, :], -1.0, None, ALU.add))

            def make_sel(col):
                dve.tensor_scalar(sel[:, 0, :], iota[:, :], pos[:, 0, bass.ds(col, 1)], None, ALU.is_equal)
                dve.tensor_scalar(sel[:, 1, :], iota[:, :], pos[:, 1, bass.ds(col, 1)], None, ALU.is_equal)\
                   .then_inc(sel_ready, 1)

            make_sel(0)
            dve.wait_ge(exp_top, 1)
            link(dve.tensor_scalar(wts[:, :, 0], wts[:, :, 1], 1.0, None, ALU.add))
            link(dve.reciprocal(wts[:, :, 0], wts[:, :, 0]))
            link(dve.tensor_tensor(wts[:, :, 1], wts[:, :, 1], wts[:, :, 0], ALU.mult))
            dve.tensor_tensor(wtab[:, :, 0:EXPERTS], pick[:, :, :], wts[:, :, 0:1].to_broadcast((P, TT, EXPERTS)), ALU.mult)
            link(dve.tensor_tensor(tmp8[:, :, :], pick2[:, :, :], wts[:, :, 1:2].to_broadcast((P, TT, EXPERTS)), ALU.mult))
            link(dve.tensor_tensor(wtab[:, :, 0:EXPERTS], wtab[:, :, 0:EXPERTS], tmp8[:, :, :], ALU.add))
            HF = FF // 256

            def overflow_ranks():
                link(dve.tensor_scalar(ov[:, :], cnt[:, :], float(P), None, ALU.is_gt))
                link(dve.memset(rank[:, :, :], 0.0))
                link(dve.tensor_copy(rank[:, 0, 1:EXPERTS], ov[:, 0:EXPERTS - 1]))
                for i, d in enumerate((1, 2, 4)):
                    a, b = i % 2, (i + 1) % 2
                    dve.tensor_copy(rank[:, b, 0:d], rank[:, a, 0:d])
                    link(dve.tensor_tensor(rank[:, b, d:EXPERTS], rank[:, a, d:EXPERTS], rank[:, a, 0:EXPERTS - d], ALU.add))
                link(dve.tensor_reduce(ovf[:, 0:1], ov[:, :], AX.X, ALU.add))

            def overflow_round(m):
                ohb = oneh[:, m:m + 1, :].to_broadcast((P, TT, EXPERTS))
                link(dve.scalar_tensor_tensor(out=oneh[:, m, :], in0=rank[:, 1, :], scalar=float(m), in1=ov[:, :],
                                              op0=ALU.is_equal, op1=ALU.mult))
                dve.tensor_tensor(cnt[:, :], oneh[:, m, :], iota8, ALU.mult)
                link(dve.tensor_tensor(tmp8[:, :, :], pos[:, :, 0:EXPERTS], ohb, ALU.mult))
                dve.tensor_reduce(ovf[:, m + 1:m + 2], cnt[:, :], AX.X, ALU.add)
                link(dve.tensor_reduce(pos[:, :, EXPERTS + m], tmp8[:, :, :], AX.X, ALU.add))
                dve.tensor_scalar(pos[:, :, EXPERTS + m], pos[:, :, EXPERTS + m], float(-P), None, ALU.add)
                link(dve.tensor_tensor(tmp8[:, :, :], wtab[:, :, 0:EXPERTS], ohb, ALU.mult))
                link(dve.tensor_reduce(wtab[:, :, EXPERTS + m], tmp8[:, :, :], AX.X, ALU.add))

            def overflow_end():
                dve.tensor_copy(ovi[:, :], ovf[:, :]).then_inc(routed, 1)
                dve.wait_ge(routed, 1)
                link(dve.tensor_scalar(ovf[:, 0:1], ovf[:, 0:1], 1.0, None, ALU.min))
                link(dve.tensor_scalar(ovf[:, 1:2], ovf[:, 0:1], -1.0, 1.0, ALU.mult, ALU.add))
                link(dve.tensor_scalar(wtab[:, :, COLS - 1], wtab[:, :, EXPERTS - 1], ovf[:, 1:2], None, ALU.mult))
                link(dve.scalar_tensor_tensor(out=wtab[:, :, COLS - 1], in0=wtab[:, :, COLS - 2], scalar=ovf[:, 0:1],
                                              in1=wtab[:, :, COLS - 1], op0=ALU.mult, op1=ALU.add))

            def expert(prev):
                plan = first if prev is None else rnd
                done_to = [SPLIT if prev is None else 0]

                def rest_to(n):
                    rest_units(prev, done_to[0], min(n, E_UNITS))
                    done_to[0] = max(done_to[0], n)

                def wait_drained(key):
                    b, n = plan.bank[key][0]
                    dve.wait_ge(drained[b], rounds(prev, first.used[b], rnd.used[b], route.used[b] + n + 1))

                def wait_step(key):
                    dve.wait_ge(step_done, rounds(prev, first.steps, rnd.steps, S0 + plan.step_no[key] + 1))

                def hidden_rest(j):
                    dve.wait_ge(hT_hi_ready, rounds(prev, GU_STEPS, GU_STEPS, j + 1))
                    b = 4 + (j + 1) % 2
                    dve.tensor_tensor(eT_lo[:, 4 * j:4 * j + 4, :], bank[b][:, :].rearrange("p (k s) -> p k s", k=4),
                                      eT_hi[:, 4 * j:4 * j + 4, :].bitcast(F32), ALU.subtract).then_inc(drained[b], 1)

                if prev is not None:
                    rest_to(2)
                    for i in range(2):
                        dve.wait_ge(y_hi_ready, prev * 2 + (i + 1))
                        dve.tensor_tensor(ye_lo[:, 512 * i:512 * i + 512], bank[6 + i][:, :],
                                          ye_hi[:, 512 * i:512 * i + 512].bitcast(F32), ALU.subtract)\
                           .then_inc(drained[6 + i], 1)
                for j in range(GU_STEPS):
                    rest_to(plan.unit_no[("u", j, 1)] + 1 + 2)
                    dve.wait_ge(unit_done, rounds(prev, E_UNITS, E_UNITS, U0 + plan.unit_no[("u", j, 1)] + 1))
                    wait_drained(("g", j, 0))
                    b, n = plan.bank[("u", j, 0)][0]
                    dve.tensor_tensor(eh[:, j % 2, :], bank[b][:, :], esilu[:, j % 2, :], ALU.mult).then_inc(drained[b], 1)
                    wait_drained(("u", j, 0))
                    dve.sem_inc(h_ready, 1)
                    if j:
                        hidden_rest(j - 1)
                    elif prev is not None:
                        for i in range(4):
                            wait_step(("combine", i))
                            dst = acc[:, i // 2, 512 * (i % 2):512 * (i % 2) + 512]
                            dve.scalar_tensor_tensor(out=dst, in0=bank[4 + i][:, :], scalar=wtab[:, i // 2, bass.ds(prev, 1)],
                                                     in1=dst, op0=ALU.mult, op1=ALU.add).then_inc(drained[4 + i], 1)
                    if prev is None and j == 2:
                        overflow_ranks()
                    if prev is None and j > 2 and j - 3 < OVER:
                        overflow_round(j - 3)
                rest_to(plan.before[("hT", GU_STEPS - 1)] + 2)
                hidden_rest(GU_STEPS - 1)
                if prev is None:
                    overflow_end()
                make_sel(1 if prev is None else prev + 2)
                rest_to(plan.before["dispatch"] + 2)
                wait_step("dispatch")
                for i in range(2):
                    dve.tensor_copy(xe_lo[:, 4 * i:4 * i + 4, :], bank[2 + i][:, :].rearrange("p (k s) -> p k s", k=4))\
                       .then_inc(drained[2 + i], 1)
                rest_to(E_UNITS)

            rest_units(None, 2, SPLIT)
            dve.wait_ge(step_done, route.step_no["dispatch"] + 1)
            for i in range(2):
                dve.tensor_copy(xe_lo[:, 4 * i:4 * i + 4, :], bank[2 + i][:, :].rearrange("p (k s) -> p k s", k=4))\
                   .then_inc(drained[2 + i], 1)
            dve.wait_ge(step_done, route.step_no["counts"] + 1)
            dve.tensor_copy(cnt[:, :], bank[5][:, 0:EXPERTS]).then_inc(drained[5], 1)
            dve.wait_ge(drained[5], route.bank["counts"][0][1] + 1)
            expert(None)
            dve.wait_ge(acc_ready, 1)
            with dve.Fori(0, EXPERTS - 1) as e:
                expert(e)
            over = dve.value_load(ovi[0:1, 0:1], min_val=0, max_val=OVER)
            with dve.If(over > 0):
                with dve.Fori(0, OVER) as m:
                    expert(m + (EXPERTS - 1))
            dve.drain().then_inc(sum_ready, 1)
            dve.wait_ge(sum_ready, 1)
            for i in range(2):
                dve.wait_ge(last_y_hi, i + 1)
                dve.tensor_tensor(ye_lo[:, 512 * i:512 * i + 512], bank[6 + i][:, :],
                                  ye_hi[:, 512 * i:512 * i + 512].bitcast(F32), ALU.subtract).then_inc(last_y, 1)
            for i in range(4):
                tile, h = divmod(i, 2)
                dve.wait_ge(last_sum, i + 1)
                dst = acc[:, tile, 512 * h:512 * h + 512]
                dve.scalar_tensor_tensor(out=dst, in0=bank[i][:, :], scalar=wtab[:, tile, COLS - 1:COLS], in1=dst,
                                         op0=ALU.mult, op1=ALU.add).then_inc(acc_done, 1)
                if i:
                    dve.wait_ge(acc_done, i)
                    dve.bn_stats(stats[:, (i - 1) // 2, (i - 1) % 2, :], last)
                last = dst
            dve.wait_ge(acc_done, 4)
            link(dve.bn_stats(stats[:, 1, 1, :], last))
            layer_norm(5, 2, acc)
            dve.wait_ge(dve_normed, 6 * DEPTH)
            dve.wait_ge(ln_loaded, 32 * 3 * DEPTH)
            link(dve.tensor_tensor(x[:, 0, :], x[:, 0, :], last_gb[:, 0, :], ALU.mult))
            dve.tensor_tensor(x[:, 0, :], x[:, 0, :], last_gb[:, 1, :], ALU.add).then_inc(ln_dve, 1)
            dve.wait_ge(act_normed, 6 * DEPTH)
            part = x[:, 1, POOL_PART:D]
            link(dve.tensor_tensor(part, part, last_gb[:, 0, POOL_PART:D], ALU.mult))
            dve.tensor_tensor(part, part, last_gb[:, 1, POOL_PART:D], ALU.add).then_inc(ln_dve, 1)

        @block.tensor
        def _(pe):
            def product3(dst, l_hi, l_lo, r_hi, r_lo, first, last):
                pe.matmul(dst, l_hi, r_hi, start=first, stop=False)
                pe.matmul(dst, l_hi, r_lo, start=False, stop=False)
                return pe.matmul(dst, l_lo, r_hi, start=False, stop=last)

            def weights(key):
                u = dense.unit_no[key]
                f = dense.units[u][1]
                return w_hi[:, u % SPLIT, 0:f], w_lo[:, u % SPLIT, 0:f]

            def begin(key):
                pe.wait_ge(lo_ready, dense.unit_no[key] + 1)
                if key in dense.bank:
                    await_banks(pe, dense.bank[key])
                hi, lo = weights(key)
                return hi, lo

            def pb(key, i=0):
                return bank[dense.bank[key][i][0]]

            def feature_form(key, a_hi, a_lo, kt=KD, tiles=2, by_tile=None):
                hi, lo = begin(key)
                hi, lo = (w.rearrange("p (k n) -> p k n", k=kt) for w in (hi, lo))
                for n in range(tiles):
                    dst = pb(key, n // 2)[:, T * (n % 2):T * (n % 2) + T]
                    for k in range(kt):
                        if by_tile and n == 0 and k % 2 == 0:
                            by_tile(k // 2)
                        wh, wl = hi[:, k, P * n:P * n + P], lo[:, k, P * n:P * n + P]
                        last = product3(dst, wh, wl, a_hi[:, k, :], a_lo[:, k, :], k == 0, k == kt - 1)
                last.then_inc(unit_done, 1)

            def token_form(key, a_hi, a_lo, by_tile=None):
                hi, lo = (w.rearrange("p (k n) -> p k n", k=KD) for w in begin(key))
                cols = hi.shape[2]
                for i in range(TT):
                    dst = pb(key)[:, cols * i:cols * i + cols]
                    for k in range(KD):
                        toks = slice(P * i, P * i + P)
                        if by_tile and i == 0 and k % 2 == 0:
                            by_tile(k // 2)
                        last = product3(dst, a_hi[:, k, toks], a_lo[:, k, toks], hi[:, k, :], lo[:, k, :],
                                        k == 0, k == KD - 1)
                last.then_inc(unit_done, 1)

            def begin_step(key):
                await_banks(pe, dense.bank[key])

            def after(key, i=0):
                b, n = dense.bank[key][i]
                pe.wait_ge(drained[b], n + 1)

            def transposes(key, src, k0):
                begin_step(key)
                for k in range(2):
                    for i in range(TT):
                        last = pe.transpose(pb(key)[:, T * k + P * i:T * k + P * i + P],
                                            src[:, i, P * (k0 + k):P * (k0 + k) + P], ident)
                last.then_inc(step_done, 1)

            def x_to_features(l, w, n=None):
                for i in range(4):
                    if n is not None and i % 2 == 0:
                        pe.wait_ge(dve_normed, 2 * n + i // 2 + 1)
                        pe.wait_ge(act_normed, 2 * n + i // 2 + 1)
                    transposes(("xT", l, w, i), x, 2 * i)

            pe.wait_ge(x_loaded, 16)
            pe.wait_ge(mats_loaded, 16)
            x_to_features(0, 0)
            begin_step("bias")
            pe.wait_ge(bias_in, 32)
            pe.matmul(pb("bias")[0:SWA_HEADS, 0:REL], table[:, :], onehot[:, :], start=True, stop=True)\
              .then_inc(step_done, 1)

            for l in range(DEPTH):
                feature_form((l, "kv"), xT_hi, xT_lo, by_tile=lambda k: after(("xT", l, 0, k)))
                token_form((l, "bk"), xT_hi, xT_lo)
                key = (l, "vT")
                begin_step(key)
                after((l, "kv"))
                for w in range(3):
                    last = pe.transpose(pb(key)[:, P * w:P * w + P], vT[:, CHUNK * w:CHUNK * w + P], ident)
                last.then_inc(step_done, 1)
                feature_form((l, "lr"), xT_hi, xT_lo, tiles=1)
                feature_form((l, "q", 0), xT_hi, xT_lo)
                feature_form((l, "q", 1), xT_hi, xT_lo)
                token_form((l, "bv", 0), xT_hi, xT_lo)
                after((l, "kv"), 0)
                after((l, "q", 0))
                after((l, "q", 1))
                for c in range(NC):
                    key = (l, "scores", c)
                    begin_step(key)
                    k0 = CHUNK * max(c - 1, 0)
                    for i in range(PAIRS):
                        last = pe.matmul(pb(key)[:, P * i:P * i + P], q_bd[:, i, c, :], kT[:, k0:k0 + P], start=True, stop=True)
                    last.then_inc(step_done, 1)
                token_form((l, "bv", 1), xT_hi, xT_lo)
                key = (l, "z")
                begin_step(key)
                pe.wait_ge(const_loaded, CONSTS)
                after((l, "lr"))
                for i in range(TT):
                    dst = pb(key)[:, T * i:T * i + T]
                    last = pe.matmul(dst, lrT[0:RANK + 1, P * i:P * i + P], alpha2[0:RANK + 1, l, :], start=True, stop=True)
                last.then_inc(step_done, 1)
                feature_form((l, "bq"), xT_hi, xT_lo)
                token_form((l, "br", 0), xT_hi, xT_lo)
                key = (l, "cum")
                begin_step(key)
                after((l, "z"))
                for i in range(TT):
                    last = pe.matmul(pb(key)[:, T * i:T * i + T], later, log_a[:, i, :], start=True, stop=True)
                last.then_inc(step_done, 1)
                key = (l, "end")
                begin_step(key)
                for p2 in range(2):
                    for i in range(TT):
                        c0 = NC * p2 + 2 * i
                        last = pe.matmul(pb(key)[:, c0:c0 + 2], log_a[:, i, P * p2:P * p2 + P], ind[:, 0:2],
                                         start=True, stop=True)
                last.then_inc(step_done, 1)
                token_form((l, "br", 1), xT_hi, xT_lo)
                pe.wait_ge(normed, l + 1)
                for c in range(NC):
                    key = (l, "pT", c)
                    begin_step(key)
                    for i in range(PAIRS):
                        last = pe.transpose(pb(key)[:, P * i:P * i + P], prob[:, c, i, :], ident)
                    last.then_inc(step_done, 1)
                feature_form((l, "cc", 0), xT_hi, xT_lo)
                pe.wait_ge(kdec_ready, 2 * l + 2)
                after((l, "bv", 0))
                after((l, "bv", 1))
                for c in range(NC):
                    key = (l, "state", c)
                    begin_step(key)
                    for p2 in range(2):
                        last = pe.matmul(pb(key)[:, T * p2:T * p2 + T], kdec[:, c % 2, c // 2, P * p2:P * p2 + P],
                                         bv[:, c // 2, T * p2:T * p2 + T], start=True, stop=True)
                    last.then_inc(step_done, 1)
                feature_form((l, "cc", 1), xT_hi, xT_lo)
                after((l, "vT"))
                for c in range(NC):
                    key = (l, "pv", c)
                    begin_step(key)
                    after((l, "pT", c))
                    pe.matmul(pb(key)[:, :], vwin[:, max(c - 1, 0), :], probT[:, c, :], start=True, stop=True)\
                      .then_inc(step_done, 1)
                feature_form((l, "ch", 0), xT_hi, xT_lo)
                after((l, "bq"))
                pe.wait_ge(state_ready, NC * (l + 1))
                for i in range(TT):
                    key = (l, "gla", i)
                    begin_step(key)
                    for h in range(2):
                        c = 2 * i + h
                        for p2 in range(2):
                            last = pe.matmul(pb(key)[64 * h:64 * h + 64, T * p2:T * p2 + T],
                                             bqT[:, p2, CHUNK * c:CHUNK * c + CHUNK], state[:, c, p2, :],
                                             start=True, stop=True)
                    last.then_inc(step_done, 1)
                feature_form((l, "ch", 1), xT_hi, xT_lo)
                feature_form((l, "cb", 0), xT_hi, xT_lo)
                feature_form((l, "cb", 1), xT_hi, xT_lo)
                pe.wait_ge(yb_ready, l + 1)
                for i in range(2):
                    transposes((l, "ybT", i), gla, 2 * i)
                for half in range(2):
                    for b in range(3):
                        for i in range(2):
                            feature_form((l, "gate", half, b, i), xT_hi, xT_lo)
                        if half == 0 and b == 0:
                            after((l, "pv", NC - 1))
                        if half == 0 and b == 1:
                            after((l, "ybT", 0))
                            after((l, "ybT", 1))
                        if half == 0 and b == 2:
                            pe.wait_ge(y_ready, l + 1)
                        feature_form((l, "branch", half, b), y_hi[:, b], y_lo[:, b], kt=KB, tiles=4)
                pe.wait_ge(mem_loaded, 16 * (l + 1))
                for n in range(4):
                    transposes((l, "memT", n), mem_tok, 2 * n)
                for n in range(4):
                    token_form((l, "out", n), merged_hi, merged_lo,
                               (lambda k: pe.wait_ge(merged_ready, 4 * l + k + 1)) if n == 0 else None)
                for n in range(l, 4):
                    feature_form((l, "xk", n), memT_hi, memT_lo, by_tile=(lambda k: after((l, "memT", k))) if n == l else None)
                x_to_features(l, 1, 3 * l)
                for n in range(2):
                    token_form((l, "xv", n), memT_hi, memT_lo)
                for i in range(4):
                    after(("xT", l, 1, i))

                def xattn_scores(h):
                    key = (l, "xs", h)
                    begin_step(key)
                    after((l, "xq", h))
                    after((l, "xk", h))
                    keys = xk_early if (l, h) == (1, 0) else xkT[:, 2 * h:2 * h + 2, :]
                    for i in range(TT):
                        for k in range(2):
                            last = pe.matmul(pb(key)[:, T * i:T * i + T], xqT[:, 2 * h + k, P * i:P * i + P],
                                             keys[:, k, :], start=(k == 0), stop=(k == 1))
                    last.then_inc(step_done, 1)

                def xattn_probT(h):
                    key = (l, "xp", h)
                    begin_step(key)
                    pe.wait_ge(xprob_ready, 4 * l + h + 1)
                    for m in range(2):
                        for i in range(TT):
                            last = pe.transpose(pb(key)[:, T * m + P * i:T * m + P * i + P],
                                                xprob[:, h, i, P * m:P * m + P], ident)
                    last.then_inc(step_done, 1)

                def xattn_out(h):
                    key = (l, "xo", h)
                    begin_step(key)
                    after((l, "xp", h))
                    after((l, "xv", h))
                    for k in range(2):
                        for m in range(2):
                            last = pe.matmul(pb(key)[:, T * k:T * k + T], xv[:, m, 256 * h + P * k:256 * h + P * k + P],
                                             xprobT[:, h, m, :], start=(m == 0), stop=(m == 1))
                    last.then_inc(step_done, 1)

                feature_form((l, "xq", 0), xT_hi, xT_lo)
                feature_form((l, "xq", 1), xT_hi, xT_lo)
                xattn_scores(0)
                feature_form((l, "xq", 2), xT_hi, xT_lo)
                xattn_scores(1)
                xattn_probT(0)
                feature_form((l, "xq", 3), xT_hi, xT_lo)
                xattn_scores(2)
                xattn_probT(1)
                xattn_out(0)
                token_form((l, "xv", 2), memT_hi, memT_lo)
                xattn_scores(3)
                xattn_probT(2)
                xattn_out(1)
                token_form((l, "xv", 3), memT_hi, memT_lo)
                xattn_probT(3)
                xattn_out(2)
                xattn_out(3)
                for n in range(4):
                    token_form((l, "xw", n), xoT_hi, xoT_lo, (lambda h: after((l, "xo", h))) if n == 0 else None)
                if l == 0:
                    feature_form((1, "xk", 0), memT_hi, memT_lo)
                x_to_features(l, 2, 3 * l + 1)
                if l:
                    continue
                for n in range(FF // 256):
                    feature_form((l, "fg", n), xT_hi, xT_lo, by_tile=(lambda k: after(("xT", l, 2, k))) if n == 0 else None)
                    feature_form((l, "fu", n), xT_hi, xT_lo)
                key = (l, "ffn")
                await_banks(pe, dense.bank[key])
                for n in range(FF // 256):
                    pe.wait_ge(h_ready, n + 1)
                    hi, lo = (w.rearrange("p (k n) -> p k n", k=2) for w in begin((l, "fd", n)))
                    for i in range(TT):
                        toks = slice(P * i, P * i + P)
                        for h in range(2):
                            cols = slice(512 * h, 512 * h + 512)
                            for k in range(2):
                                kk = 2 * n + k
                                last = product3(pb(key, 2 * i + h)[:, :], hT_hi[:, kk, toks], hT_lo[:, kk, toks],
                                                hi[:, k, cols], lo[:, k, cols], kk == 0, kk == NF - 1)
                            if n == FF // 256 - 1 and (i, h) != (1, 1):
                                last.then_inc(ffn_done, 1)
                    last.then_inc(unit_done, 1)
                x_to_features(1, 0, 2)

            for b, n in route.bank["logits"]:
                pe.wait_ge(drained[b], n)
            pe.wait_ge(router_ready, 1)
            E = EXPERTS
            for k in range(KD):
                if k % 2 == 0:
                    after(("xT", 1, 2, k // 2))
                for i in range(TT):
                    toks = slice(P * i, P * i + P)
                    b = route.bank["logits"][i][0]
                    pe.matmul(bank[b][:, 0:2 * E], xT_hi[:, k, toks],
                              w_rt2[:, k, :, :].rearrange("p a e -> p (a e)"), start=(k == 0), stop=False)
                    last = pe.matmul(bank[b][:, 0:E], xT_lo[:, k, toks], w_rt2[:, k, 0, :],
                                     start=False, stop=(k == KD - 1))
            last.then_inc(step_done, 1)
            b, n = route.bank["ranks"][0]
            pe.wait_ge(drained[b], n)
            pe.wait_ge(picked_ready, 1)
            pe.matmul(bank[b][:, 0:E], earlier, picked[:, 0, :], start=True, stop=True)
            pe.matmul(bank[b][:, E:2 * E], earlier, picked[:, 1, :], start=True, stop=False)
            pe.matmul(bank[b][:, E:2 * E], ones[:, :], picked[:, 0, :], start=False, stop=True).then_inc(step_done, 1)

            def dispatch():
                for part, src in enumerate((xtok_hi, xtok_lo)):
                    for k in range(KD):
                        dst = bank[2 * part + k // 4][:, P * (k % 4):P * (k % 4) + P]
                        for i in range(TT):
                            last = pe.matmul(dst, src[:, i, P * k:P * k + P], sel[:, i, :], start=(i == 0), stop=(i == TT - 1))
                last.then_inc(step_done, 1)

            for b, n in route.bank["dispatch"]:
                pe.wait_ge(drained[b], n)
            pe.wait_ge(xtok_ready, 1)
            pe.wait_ge(sel_ready, 1)
            dispatch()
            b, n = route.bank["counts"][0]
            pe.wait_ge(drained[b], n)
            pe.matmul(bank[b][:, 0:E], ones[:, :], picked[:, 0, :], start=True, stop=False)
            pe.matmul(bank[b][:, 0:E], ones[:, :], picked[:, 1, :], start=False, stop=True).then_inc(step_done, 1)

            def combine(i, b):
                tile, half = divmod(i, 2)
                cols = slice(512 * half, 512 * half + 512)
                pe.matmul(bank[b][:, :], selT[:, tile, :], ye_hi[:, cols], start=True, stop=False)
                return pe.matmul(bank[b][:, :], selT[:, tile, :], ye_lo[:, cols], start=False, stop=True)

            def expert(prev):
                plan = first if prev is None else rnd

                def drained_to(b, n):
                    pe.wait_ge(drained[b], rounds(prev, first.used[b], rnd.used[b], route.used[b] + n))

                def unit(key):
                    i = plan.unit_no[key]
                    pe.wait_ge(lo_ready, rounds(prev, E_UNITS, E_UNITS, U0 + i + 1))
                    s = (U0 + i) % SPLIT
                    kt = 2 if key[0] == "d" else 4
                    return (w[:, s, :].rearrange("p (k n) -> p k n", k=kt) for w in (w_hi, w_lo))

                def columns(name, j):
                    b, n = plan.bank[(name, j, 0)][0]
                    for half in range(2):
                        hi, lo = unit((name, j, half))
                        if half == 0:
                            drained_to(b, n)
                        for k in range(4):
                            kk = 4 * half + k
                            last = product3(bank[b][:, :], xe_hi[:, kk, :], xe_lo[:, kk, :], hi[:, k, :], lo[:, k, :],
                                            kk == 0, kk == KD - 1)
                        last.then_inc(unit_done, 1)

                def hidden_transposes(j):
                    b, n = plan.bank[("hT", j)][0]
                    drained_to(b, n)
                    pe.wait_ge(h_ready, rounds(prev, GU_STEPS, GU_STEPS, FF // 256 + j + 1))
                    for k in range(4):
                        last = pe.transpose(bank[b][:, P * k:P * k + P], eh[:, j % 2, P * k:P * k + P], ident)
                    last.then_inc(step_done, 1)

                for i in range(4):
                    drained_to(i, 0)
                for j in range(GU_STEPS):
                    columns("g", j)
                    columns("u", j)
                    if j:
                        hidden_transposes(j - 1)
                    elif prev is not None:
                        for b, m in plan.bank["y"]:
                            drained_to(b, 0)
                        for i in range(4):
                            b, m = plan.bank[("combine", i)][0]
                            drained_to(b, m)
                            combine(i, b).then_inc(step_done, 1)
                    if j == 1:
                        b, n = plan.bank["selT"][0]
                        drained_to(b, n)
                        for i in range(TT):
                            last = pe.transpose(bank[b][:, P * i:P * i + P], sel[:, i, :].bitcast(F32), ident)
                        last.then_inc(step_done, 1)
                for n in range(D_UNITS):
                    hi, lo = unit(("d", n))
                    if n == 0:
                        for b, m in plan.bank["y"]:
                            drained_to(b, m)
                    if n % 2 == 0:
                        b, m = plan.bank[("hT", n // 2)][0]
                        drained_to(b, m + 1)
                    for k in range(2):
                        kk = 2 * n + k
                        for h in range(2):
                            cols = slice(512 * h, 512 * h + 512)
                            last = product3(bank[6 + h][:, :], eT_hi[:, kk, :], eT_lo[:, kk, :], hi[:, k, cols], lo[:, k, cols],
                                            kk == 0, kk == EK - 1)
                    last.then_inc(unit_done, 1)
                    if n == 1:
                        hidden_transposes(GU_STEPS - 1)
                    if n == 7:
                        for b, m in plan.bank["dispatch"]:
                            drained_to(b, m)
                        pe.wait_ge(sel_ready, 2 if prev is None else prev + 3)
                        dispatch()

            expert(None)
            with pe.Fori(0, EXPERTS - 1) as e:
                expert(e)
            pe.wait_ge(routed, 1)
            over = pe.value_load(ovi[0:1, 0:1], min_val=0, max_val=OVER)
            with pe.If(over > 0):
                with pe.Fori(0, OVER) as m:
                    expert(m + (EXPERTS - 1))
            pe.drain().then_inc(rounds_done, 1)
            pe.wait_ge(last_y, 2)
            for i in range(4):
                combine(i, i).then_inc(last_sum, 1)


def shape_constants():
    import numpy as np

    n = np.arange(P)
    same = n[:, None] // CHUNK == n[None, :] // CHUNK
    mats = np.stack([np.eye(P), (same & (n[:, None] > n[None, :])) / 16.0, n[:, None] < n[None, :]])
    ind = np.zeros((P, 4))
    for g in range(2):
        ind[CHUNK * g:CHUNK * g + CHUNK, g] = 1 / 16.0
        ind[CHUNK * g:CHUNK * g + CHUNK, 2 + g] = 1.0
    rel = np.arange(-(P - 1), CHUNK)
    half, exact = BUCKETS // 2, BUCKETS // 4
    a = np.abs(rel)
    large = exact + (np.log(np.maximum(a, 1) / exact) / np.log(128 / exact) * (half - exact)).astype(np.int32)
    bucket = (rel > 0) * half + np.where(a < exact, a, np.minimum(large, half - 1))
    onehot = np.zeros((BUCKETS, REL))
    onehot[bucket, np.arange(len(rel))] = 1.0
    return {"c_mats": mats.astype(np.float32), "c_ind": ind.astype(np.float32),
            "c_onehot": onehot.astype(np.float32), "c_iota": np.arange(P, dtype=np.float32)[None, :]}


_INS = ["x", "mem", "w_in", "b_merge", "attn_sink", "rel_bias", "w_alpha2", "b_alpha2", "gla_gain", "conv_w",
        "w_branch", "w_out", "ln1_g", "ln1_b", "w_xq", "w_xkv", "w_xo", "ln2_g", "ln2_b", "w_ff_gu", "w_ff_d",
        "w_router", "b_router", "w_e_gu", "w_e_d", "ln3_g", "ln3_b"]


def kernel(**inputs):
    import numpy as np
    import concourse.bacc as bacc
    from concourse.bass_utils import run_bass_kernel_spmd as run

    nc = bacc.Bacc("TRN2", target_bir_lowering=False, num_devices=1)
    arrays = {name: np.ascontiguousarray(inputs[name]) for name in _INS}
    arrays["conv_w"] = np.ascontiguousarray(arrays["conv_w"].reshape(DEPTH, 3, KB, P).transpose(3, 0, 1, 2))
    arrays["b_merge"] = np.ascontiguousarray(arrays["b_merge"].reshape(DEPTH, 3 * KD, P).transpose(2, 0, 1))
    arrays["ln_f"] = np.ascontiguousarray(np.stack([
        np.stack([arrays[f"ln{w}_{v}"] for w in (1, 2, 3)], 1).reshape(3 * DEPTH, KD, P) for v in "gb"]).transpose(3, 0, 1, 2))
    arrays.update(shape_constants())
    t = {name: nc.dram_tensor(name, a.shape, mybir.dt.from_np(a.dtype), kind="ExternalInput").ap()
         for name, a in arrays.items()}
    scratch = nc.dram_tensor("bias_by_offset", (SWA_HEADS * CHUNK * REL,), F32).ap()
    out = nc.dram_tensor("out", (1, T, D), F32, kind="ExternalOutput").ap()
    hybrid_layers(nc, t, scratch, out)
    r = run(nc, [arrays], core_ids=[0])
    return r.results[0]["out"]
```
